# Optimizing a Trainium2 kernel written in Bass

```python
import jax, jax.numpy as jnp
from jax import lax
import numpy as np

D_MODEL = 1024
BATCH = 1
SEQ = 256
DEPTH = 2

N_META = 16
NORM_EPS = 1e-6
RWKV_HEADS = 8
RWKV_HEAD_DIM = 64
RWKV_WIDTH = RWKV_HEADS * RWKV_HEAD_DIM
LORA_W = 64
LORA_A = 64
LORA_G = 128
RWKV_IN = 3 * RWKV_WIDTH + LORA_W + LORA_A + LORA_G
GN_EPS = 64e-5
LRU_BLOCKS = 8
LRU_BLOCK = 64
LRU_WIDTH = LRU_BLOCKS * LRU_BLOCK
CONV_WIDTH = 4
LRU_C = 8.0
EVEN_IN = RWKV_IN + 2 * LRU_WIDTH
EVEN_MIX = RWKV_WIDTH + LRU_WIDTH
GLA_HEADS = 4
GLA_DK = 128
GLA_DV = 256
GLA_KEY_WIDTH = GLA_HEADS * GLA_DK
GLA_VAL_WIDTH = GLA_HEADS * GLA_DV
GLA_LORA = 16
GLA_TAU = 16.0
GLA_CHUNK = 64
ODD_IN = 2 * GLA_KEY_WIDTH + 2 * GLA_VAL_WIDTH + GLA_LORA
N_GROUPS = 4
EXPERTS_PER_GROUP = 8
N_EXPERTS = N_GROUPS * EXPERTS_PER_GROUP
TOP_K = 2
EXPERT_FF = 256
N_EVEN = (DEPTH + 1) // 2
N_ODD = DEPTH // 2

kernel_name = 'hybrid_rwkv7_rglru_gla_hmoe'

def rms_norm(x, gain):
    xf = x.astype(jnp.float32)
    y = xf * lax.rsqrt(jnp.mean(xf * xf, axis=-1, keepdims=True) + NORM_EPS)
    return (y * gain.astype(jnp.float32)).astype(x.dtype)

def token_shift(p):
    return jnp.pad(p, ((0, 0), (1, 0), (0, 0)))[:, :-1]

def rwkv7_mix(p, mu, decay0, decay_up, iclr0, iclr_up, gate_up, k_k, k_a, r_k, ln_g, ln_b):
    B, T, _ = p.shape
    f32 = jnp.float32
    H, Dh, W = RWKV_HEADS, RWKV_HEAD_DIM, RWKV_WIDTH
    p = p + mu * (token_shift(p) - p)
    r, k, v, wd, ad, gd = jnp.split(p, [W, 2 * W, 3 * W, 3 * W + LORA_W, 3 * W + LORA_W + LORA_A], axis=-1)
    w = -jax.nn.softplus(-(decay0 + jnp.tanh(wd) @ decay_up).astype(f32)) - 0.5
    decay = jnp.exp(-jnp.exp(w))
    a = jax.nn.sigmoid((iclr0 + ad @ iclr_up).astype(f32))
    g = (jax.nn.sigmoid(gd) @ gate_up).astype(f32)
    heads = lambda t: t.reshape(B, T, H, Dh)
    kk = heads((k * k_k).astype(f32))
    kk = kk / jnp.maximum(jnp.linalg.norm(kk, axis=-1, keepdims=True), 1e-12)
    k_mod = k.astype(f32) * (1.0 + (a - 1.0) * k_a.astype(f32))
    r_h, k_h, v_h, a_h, w_h = heads(r.astype(f32)), heads(k_mod), heads(v.astype(f32)), heads(a), heads(decay)
    tm = lambda t: jnp.moveaxis(t, 1, 0)

    def step(S, inp):
        r_t, w_t, k_t, v_t, kk_t, b_t = inp
        sa = jnp.einsum('bhvk,bhk->bhv', S, kk_t)
        S = S * w_t[:, :, None, :] - sa[..., None] * b_t[:, :, None, :] + v_t[..., None] * k_t[:, :, None, :]
        return S, jnp.einsum('bhvk,bhk->bhv', S, r_t)

    S0 = jnp.zeros((B, H, Dh, Dh), f32)
    _, o = lax.scan(step, S0, (tm(r_h), tm(w_h), tm(k_h), tm(v_h), tm(kk), tm(kk * a_h)))
    o = jnp.moveaxis(o, 0, 1)
    mean = jnp.mean(o, axis=-1, keepdims=True)
    var = jnp.mean(jnp.square(o - mean), axis=-1, keepdims=True)
    o = ((o - mean) * lax.rsqrt(var + GN_EPS)).reshape(B, T, W) * ln_g.astype(f32) + ln_b.astype(f32)
    bonus = jnp.sum(r_h * k_h * r_k.astype(f32).reshape(H, Dh), axis=-1, keepdims=True) * v_h
    o = (o + bonus.reshape(B, T, W)) * g
    return o.astype(p.dtype)

def rglru_mix(xb, gb, conv_w, conv_b, wa, ba, wx, bx, lam):
    B, T, C = xb.shape
    f32 = jnp.float32
    xc = lax.conv_general_dilated(xb, conv_w[:, None, :], window_strides=(1,),
                                  padding=[(CONV_WIDTH - 1, 0)],
                                  dimension_numbers=('NWC', 'WIO', 'NWC'),
                                  feature_group_count=C) + conv_b
    blocks = xc.reshape(B, T, LRU_BLOCKS, LRU_BLOCK)
    gate_r = jax.nn.sigmoid((jnp.einsum('btni,nij->btnj', blocks, wa).reshape(B, T, C) + ba).astype(f32))
    gate_i = jax.nn.sigmoid((jnp.einsum('btni,nij->btnj', blocks, wx).reshape(B, T, C) + bx).astype(f32))
    log_a = -LRU_C * gate_r * jax.nn.softplus(-lam.astype(f32))
    a = jnp.exp(log_a)
    u = jnp.sqrt(-jnp.expm1(2.0 * log_a)) * gate_i * xc.astype(f32)

    def combine(left, right):
        al, bl = left
        ar, br = right
        return al * ar, ar * bl + br

    _, h = lax.associative_scan(combine, (a, u), axis=1)
    return (h * jax.nn.gelu(gb.astype(f32))).astype(xb.dtype)

def gla_chunk(state, q, k, v, log_a):
    L = q.shape[2]
    cum = jnp.cumsum(log_a, axis=2)
    causal = jnp.tril(jnp.ones((L, L), dtype=bool))
    diff = cum[:, :, :, None, :] - cum[:, :, None, :, :]
    decay = jnp.where(causal[:, :, None], jnp.exp(jnp.minimum(diff, 0.0)), 0.0)
    scores = jnp.einsum('bhtk,bhsk,bhtsk->bhts', q, k, decay)
    out = jnp.einsum('bhts,bhsv->bhtv', scores, v) + jnp.einsum('bhtk,bhkv->bhtv', q * jnp.exp(cum), state)
    last = cum[:, :, -1:, :]
    new_state = state * jnp.exp(last)[:, :, 0, :, None] + jnp.einsum('bhsk,bhsv->bhkv', k * jnp.exp(last - cum), v)
    return new_state, out

def gla_mix(p, g_up, g_b, head_gain):
    B, T, _ = p.shape
    f32 = jnp.float32
    kw, vw = GLA_KEY_WIDTH, GLA_VAL_WIDTH
    q, k, v, gd, r = jnp.split(p, [kw, 2 * kw, 2 * kw + vw, 2 * kw + vw + GLA_LORA], axis=-1)
    log_a = jax.nn.log_sigmoid((gd @ g_up + g_b).astype(f32)) / GLA_TAU
    heads = lambda t, d: jnp.transpose(t.astype(f32).reshape(B, T, GLA_HEADS, d), (0, 2, 1, 3))
    q = heads(q, GLA_DK) * (GLA_DK ** -0.5)
    k = heads(k, GLA_DK)
    v = heads(v, GLA_DV)
    log_a = heads(log_a, GLA_DK)
    state = jnp.zeros((B, GLA_HEADS, GLA_DK, GLA_DV), f32)
    state, out_meta = gla_chunk(state, q[:, :, :N_META], k[:, :, :N_META], v[:, :, :N_META], log_a[:, :, :N_META])
    n_chunks = (T - N_META) // GLA_CHUNK
    chunked = lambda t: jnp.moveaxis(t[:, :, N_META:].reshape(B, GLA_HEADS, n_chunks, GLA_CHUNK, t.shape[-1]), 2, 0)
    _, out_rest = lax.scan(lambda s, c: gla_chunk(s, *c), state, (chunked(q), chunked(k), chunked(v), chunked(log_a)))
    out_rest = jnp.moveaxis(out_rest, 0, 2).reshape(B, GLA_HEADS, T - N_META, GLA_DV)
    o = jnp.concatenate([out_meta, out_rest], axis=2).transpose(0, 2, 1, 3)
    o = o * lax.rsqrt(jnp.mean(o * o, axis=-1, keepdims=True) + NORM_EPS)
    o = o.reshape(B, T, vw) * head_gain.astype(f32) * jax.nn.silu(r.astype(f32))
    return o.astype(p.dtype)

def hier_moe(h, w_group, b_group, w_router, b_router, w_gate, w_up, w_down):
    B, T, D = h.shape
    hf = h.reshape(B * T, D)
    g_logits = (hf @ w_group + b_group).astype(jnp.float32)
    g_idx = jnp.argmax(g_logits, axis=-1)
    g_prob = jnp.take_along_axis(jax.nn.softmax(g_logits, axis=-1), g_idx[:, None], axis=-1)
    e_logits = (hf @ w_router + b_router).astype(jnp.float32).reshape(-1, N_GROUPS, EXPERTS_PER_GROUP)
    e_logits = jnp.take_along_axis(e_logits, g_idx[:, None, None], axis=1)[:, 0]
    top_val, top_idx = lax.top_k(e_logits, TOP_K)
    weights = jax.nn.softmax(top_val, axis=-1) * g_prob
    expert_idx = g_idx[:, None] * EXPERTS_PER_GROUP + top_idx
    combine = jnp.sum(jax.nn.one_hot(expert_idx, N_EXPERTS, dtype=jnp.float32) * weights[..., None], axis=1).astype(h.dtype)
    y = jnp.zeros_like(hf)
    for e in range(N_EXPERTS):
        hid = jax.nn.silu(hf @ w_gate[e]) * (hf @ w_up[e])
        y = y + (hid @ w_down[e]) * combine[:, e:e + 1]
    return y.reshape(B, T, D)

def setup_inputs(seed: int = 0) -> dict:
    key = jax.random.key(seed)
    ks = iter(jax.random.split(key, 48))
    nrm = lambda shape, scale: jax.random.normal(next(ks), shape, jnp.float32) * scale
    unif = lambda shape, lo, hi: jax.random.uniform(next(ks), shape, jnp.float32, lo, hi)
    E, O, Ld, D = N_EVEN, N_ODD, DEPTH, D_MODEL
    a_pow = unif((E, LRU_WIDTH), 0.9, 0.999) ** (1.0 / LRU_C)
    return {
        'x': nrm((BATCH, SEQ, D), 1.0),
        'meta': nrm((N_META, D), 1.0),
        'e_norm': 1.0 + nrm((E, D), 0.02),
        'e_w_in': nrm((E, D, EVEN_IN), D ** -0.5),
        'e_mu': unif((E, RWKV_IN), 0.0, 1.0),
        'e_decay0': unif((E, RWKV_WIDTH), -6.0, -1.0),
        'e_decay_up': nrm((E, LORA_W, RWKV_WIDTH), 0.1 * LORA_W ** -0.5),
        'e_iclr0': nrm((E, RWKV_WIDTH), 0.5),
        'e_iclr_up': nrm((E, LORA_A, RWKV_WIDTH), 0.1 * LORA_A ** -0.5),
        'e_gate_up': nrm((E, LORA_G, RWKV_WIDTH), LORA_G ** -0.5),
        'e_k_k': 0.85 + nrm((E, RWKV_WIDTH), 0.02),
        'e_k_a': 1.0 + nrm((E, RWKV_WIDTH), 0.02),
        'e_r_k': nrm((E, RWKV_WIDTH), 0.1),
        'e_ln_g': 1.0 + nrm((E, RWKV_WIDTH), 0.02),
        'e_ln_b': nrm((E, RWKV_WIDTH), 0.01),
        'e_conv_w': nrm((E, CONV_WIDTH, LRU_WIDTH), CONV_WIDTH ** -0.5),
        'e_conv_b': nrm((E, LRU_WIDTH), 0.01),
        'e_lru_wa': nrm((E, LRU_BLOCKS, LRU_BLOCK, LRU_BLOCK), LRU_BLOCK ** -0.5),
        'e_lru_ba': nrm((E, LRU_WIDTH), 0.01),
        'e_lru_wx': nrm((E, LRU_BLOCKS, LRU_BLOCK, LRU_BLOCK), LRU_BLOCK ** -0.5),
        'e_lru_bx': nrm((E, LRU_WIDTH), 0.01),
        'e_lru_lambda': jnp.log(a_pow) - jnp.log1p(-a_pow),
        'e_w_out': nrm((E, EVEN_MIX, D), EVEN_MIX ** -0.5),
        'o_norm': 1.0 + nrm((O, D), 0.02),
        'o_w_in': nrm((O, D, ODD_IN), D ** -0.5),
        'o_g_up': nrm((O, GLA_LORA, GLA_KEY_WIDTH), GLA_LORA ** -0.5),
        'o_g_b': nrm((O, GLA_KEY_WIDTH), 0.1),
        'o_head_gain': 1.0 + nrm((O, GLA_VAL_WIDTH), 0.02),
        'o_w_out': nrm((O, GLA_VAL_WIDTH, D), GLA_VAL_WIDTH ** -0.5),
        'm_norm': 1.0 + nrm((Ld, D), 0.02),
        'm_w_group': nrm((Ld, D, N_GROUPS), D ** -0.5),
        'm_b_group': nrm((Ld, N_GROUPS), 0.01),
        'm_w_router': nrm((Ld, D, N_EXPERTS), D ** -0.5),
        'm_b_router': nrm((Ld, N_EXPERTS), 0.01),
        'm_w_gate': nrm((Ld, N_EXPERTS, D, EXPERT_FF), D ** -0.5),
        'm_w_up': nrm((Ld, N_EXPERTS, D, EXPERT_FF), D ** -0.5),
        'm_w_down': nrm((Ld, N_EXPERTS, EXPERT_FF, D), EXPERT_FF ** -0.5),
        'final_norm': 1.0 + nrm((D,), 0.02),
    }

def reference(x, meta, e_norm, e_w_in, e_mu, e_decay0, e_decay_up, e_iclr0, e_iclr_up, e_gate_up,
              e_k_k, e_k_a, e_r_k, e_ln_g, e_ln_b, e_conv_w, e_conv_b, e_lru_wa, e_lru_ba, e_lru_wx,
              e_lru_bx, e_lru_lambda, e_w_out, o_norm, o_w_in, o_g_up, o_g_b, o_head_gain, o_w_out,
              m_norm, m_w_group, m_b_group, m_w_router, m_b_router, m_w_gate, m_w_up, m_w_down,
              final_norm):
    B = x.shape[0]
    h = jnp.concatenate([jnp.broadcast_to(meta[None].astype(x.dtype), (B, N_META, x.shape[-1])), x], axis=1)
    for layer in range(DEPTH):
        i = layer // 2
        if layer % 2 == 0:
            p = rms_norm(h, e_norm[i]) @ e_w_in[i]
            y_a = rwkv7_mix(p[..., :RWKV_IN], e_mu[i], e_decay0[i], e_decay_up[i], e_iclr0[i], e_iclr_up[i],
                            e_gate_up[i], e_k_k[i], e_k_a[i], e_r_k[i], e_ln_g[i], e_ln_b[i])
            y_b = rglru_mix(p[..., RWKV_IN:RWKV_IN + LRU_WIDTH], p[..., RWKV_IN + LRU_WIDTH:],
                            e_conv_w[i], e_conv_b[i], e_lru_wa[i], e_lru_ba[i], e_lru_wx[i], e_lru_bx[i],
                            e_lru_lambda[i])
            h = h + jnp.concatenate([y_a, y_b], axis=-1) @ e_w_out[i]
        else:
            p = rms_norm(h, o_norm[i]) @ o_w_in[i]
            h = h + gla_mix(p, o_g_up[i], o_g_b[i], o_head_gain[i]) @ o_w_out[i]
        h = h + hier_moe(rms_norm(h, m_norm[layer]), m_w_group[layer], m_b_group[layer], m_w_router[layer],
                         m_b_router[layer], m_w_gate[layer], m_w_up[layer], m_w_down[layer])
    return rms_norm(h[:, N_META:], final_norm)


_drawn_inputs = setup_inputs


def setup_inputs(seed=0):
    import zlib

    import numpy as np

    out = dict(_drawn_inputs(seed))
    spreads = {}
    factors = {'e_decay_up': 5.73,
     'e_lru_ba': 22.43,
     'e_lru_bx': 5.128,
     'o_head_gain': 7.968,
     'm_b_router': 3.146,
     'final_norm': 7.386,
     'e_k_k': 2.969,
     'e_ln_b': 2.936}
    for name, (base, spread) in spreads.items():
        noise = np.random.default_rng([zlib.crc32(name.encode()), seed]).standard_normal(out[name].shape)
        drawn = base * np.exp(spread * noise) if base else spread * noise
        out[name] = __import__('jax').numpy.asarray(drawn.astype(out[name].dtype))
    for name, factor in factors.items():
        out[name] = (out[name] * factor).astype(out[name].dtype)
    return out
```

```python
from contextlib import ExitStack

import concourse.bass as bass
from concourse import mybir

ALU = mybir.AluOpType
ACT = mybir.ActivationFunctionType
AXX = mybir.AxisListType.X
F32 = mybir.dt.float32
BF16 = mybir.dt.bfloat16
I32 = mybir.dt.int32
U32 = mybir.dt.uint32

P = 128
D = 1024
KD = D // P
META = 16
SEQ = 256
T = META + SEQ
L = 64
NC = 5
TP = NC * L
PAD = TP - T
EPS = 1e-6
GN_EPS = 64e-5
E_IN = 2816
O_IN = 3088
NE = 32
NG = 4
FF = 256
NPAIR = NE // 2
SLOTS = 64
SLAB = 4 * TP
FAR = 4096.0
TILES = [(META, P), (META + P, P), (0, META)]
PV = {}
_at = 0
for _name, _rows in (("mu", 14), ("decay0", 4), ("iclr0", 4), ("k_k", 4), ("k_a", 4), ("r_k", 4), ("ln_g", 4),
                     ("ln_b", 4), ("conv_w", 16), ("conv_b", 4), ("ba", 4), ("bx", 4), ("lam", 4), ("g_b", 4),
                     ("gain", 8)):
    PV[_name] = _at
    _at += _rows
NPV = _at
O_GROUPS = [(2048, 16), (0, 256), (256, 256), (512, 256), (768, 256)] + [(1024 + 256 * i, 256) for i in range(4)] \
    + [(2064 + 256 * i, 256) for i in range(4)]
E_TILES = [14, 15, 16, 17, 18, 19, 20, 21, 12, 13, 4, 5, 6, 7, 0, 1, 2, 3, 8, 9, 10, 11]


def program(nc, a, out, xn_dram, y_dram, upto=9):
    ctx = ExitStack()
    with ctx:
        def sb(name, shape, dt=F32):
            return ctx.enter_context(nc.sbuf_tensor(name, shape, dt))

        def sem(name):
            return ctx.enter_context(nc.semaphore(name))

        ps = ctx.enter_context(nc.psum_tensor("ps", [P, 8, 512], F32))
        RA = sb("RA", [P, 12288])
        W = sb("W", [P, 21 * SLAB])
        U = sb("U", [P, 8192])
        hT = sb("hT", [P, KD, T])
        ident = sb("ident", [P, P])
        ones = sb("ones", [P, P])
        onesbd = sb("onesbd", [P, P])
        id64 = sb("id64", [P, 64])
        before = sb("before", [P, P])
        m_ar = sb("m_ar", [P, 2, L])
        m_n = sb("m_n", [P, L])
        m_lev = sb("m_lev", [P, 6, L])
        m_lev1n = sb("m_lev1n", [P, L])
        reset = sb("reset", [P, SLAB], BF16)
        pv = sb("pv", [P, NPV])
        gains = sb("gains", [P, 4, KD])
        slam = sb("slam", [P, 8, 4])
        omka = sb("omka", [P, 4])
        epsb = sb("epsb", [P, 2])
        dlast = sb("dlast", [P, 4, NC])
        wr = sb("wr", [P, KD, NG + NE])
        np_i = sb("np_i", [P, 2], I32)
        iota_i = sb("iota_i", [P, SLOTS], I32)
        tok_i = sb("tok_i", [P, 3], I32)

        def arr(first, *dims):
            n = 1
            for d in dims:
                n *= d
            v = W[:, first * SLAB:first * SLAB + n]
            names = " ".join("abcdef"[:len(dims)])
            return v.rearrange(f"p ({names}) -> p {names}", **{"abcdef"[i]: d for i, d in enumerate(dims)}) \
                if len(dims) > 1 else v

        block = ctx.enter_context(nc.Block())
        S = {}

        def s(name):
            if name not in S:
                S[name] = sem(name)
            return S[name]

        xtok = U[:, 0:3 * D].rearrange("p (t d) -> p t d", t=3)
        xnE = arr(19, KD, T)
        rT, kT, vT, aT, LW, CUM, EX, KK, KM = (arr(i, 4, TP) for i in range(9))
        AR = arr(9, 4, NC, 2, L)
        Kt, Bt, BV, GT = (arr(i, 4, TP) for i in (11, 12, 13, 14))
        mixT = arr(15, 8, T)
        MA = arr(19, NC, 4, 2, L)
        MB = arr(17, NC, 4, 2, L)
        NN, CT = arr(0, NC, 4, L), arr(1, NC, 4, L)
        X, XT, YY = (arr(i, NC, 4, L) for i in (3, 4, 5))
        Vtk, Ktk, Btk = (arr(i, NC, 4, L) for i in (6, 7, 8))
        RH = W[:, 2 * SLAB:2 * SLAB + 256].rearrange("p (j v) -> p j v", j=4)
        nSA = W[:, 2 * SLAB + 256:2 * SLAB + 512].rearrange("p (j v) -> p j v", j=4)
        oT = arr(11, 4, TP)
        ST = W[:, 12 * SLAB:12 * SLAB + 256].rearrange("p (j v) -> p j v", j=4)
        STn = W[:, 12 * SLAB + 256:12 * SLAB + 512].rearrange("p (j v) -> p j v", j=4)
        raw = W[:, 4 * SLAB:4 * SLAB + 4 * 273].rearrange("p (s t) -> p s t", s=4)
        WA, GD, DT = (W[:, 5 * SLAB + i * T:5 * SLAB + (i + 1) * T] for i in range(3))
        rs = W[:, 6 * SLAB:6 * SLAB + T]
        xb, gb, xc, ga, gi, t1, t2, hh, aa = (arr(i, 4, T + 3 if i == 9 else T) for i in (9, 10, 11, 12, 13, 17, 18, 7, 8))
        lora = W[:, 14 * SLAB + 512:14 * SLAB + 1024]
        pvr = W[:, 14 * SLAB + 1024:14 * SLAB + 1152]
        gup = W[:, 14 * SLAB:14 * SLAB + 512]
        lruw = sb("lruw", [P, 2, 4, L])
        wring = RA[:, :].rearrange("p (s k c) -> p s k c", s=6, k=KD)
        wout = U[:, :].rearrange("p (k d) -> p k d", k=KD)
        sq = xnE

        xnO = arr(19, KD, TP)
        qO, kO = arr(0, 4, TP), arr(1, 4, TP)
        rr = arr(2, 8, T)
        Vo = arr(4, 3, D)
        rsO = W[:, 6 * SLAB + 600:6 * SLAB + 600 + T]
        LA, CU, QE, KDc, EA, QH, KH = (arr(i, 4, TP) for i in (7, 8, 9, 10, 11, 12, 13))
        EB = arr(18, 4, TP)
        PT = arr(14, 3, 4, L)
        PTt = W[:, 17 * SLAB:17 * SLAB + 768].rearrange("p (s h t) -> p s h t", s=3, h=4)
        gdT = W[0:16, 14 * SLAB + 800:14 * SLAB + 800 + T]
        kdt = arr(15, 3, 4, P)
        SG = arr(17, 4, FF)
        oG = arr(12, 8, TP)
        sqG = arr(10, 8, T)
        elast = sb("elast", [P, 4, NC])
        gupO = sb("gupO", [16, 4 * P])
        PLACE = {1: (0, 0), 2: (0, 1), 3: (1, 0), 4: (1, 1), 0: (2, 0)}

        slot_w = [RA[:, 0:12288].rearrange("p (e w) -> p e w", e=2), W[:, 0:12288].rearrange("p (e w) -> p e w", e=2)]
        xrow = U[:, 0:3 * D].rearrange("p (t d) -> p t d", t=3)
        yst = U[:, 0:2 * D].rearrange("p (s d) -> p s d", s=2)
        xg = U[:, 3072:5120].rearrange("p (s d) -> p s d", s=2)
        xgT = U[:, 5120:7168].rearrange("p (s k t) -> p s k t", s=2, k=KD)
        sil, hid = U[:, 7168:7424], U[:, 7424:7680]
        hidT = U[:, 7680:7936].rearrange("p (k t) -> p k t", k=2)
        R = W[:, 12288:18432].rearrange("p (t e c) -> p t e c", t=3, e=NE)
        yrow = W[:, 12288:18432].rearrange("p (t x d) -> p t x d", t=3, x=2)
        at = [18432]

        def rt(*dims, dt=F32):
            n = 1
            for d in dims:
                n *= d
            v = W[:, at[0]:at[0] + n]
            at[0] += n
            if dt != F32:
                v = v.bitcast(dt)
            names = " ".join("abcd"[:len(dims)])
            return v.rearrange(f"p ({names}) -> p {names}", **{"abcd"[i]: d for i, d in enumerate(dims)}) \
                if len(dims) > 1 else v

        rsM = rt(T)
        LG = rt(3, NG + NE)
        BI = rt(NG + NE)
        gmax, gsum, v1, v2, w1, w2 = (rt(3) for _ in range(6))
        eg, ohg, sg4 = rt(3, NG), rt(3, NG), rt(3, NG)
        pe4 = rt(3, NG, 8)
        el, oh1, oh2, s8 = (rt(3, 8) for _ in range(4))
        O1, O2, AA, WT, RM = (rt(3, NE) for _ in range(5))
        cnt = rt(NE)
        io = rt(SLOTS)
        tokf = rt(3)
        lims, cmp5 = rt(5), rt(5)
        cmx = rt(1)
        VV = rt(3, NPAIR, 6)
        TB = rt(NPAIR, 6)
        K2, WS, GI, SI = (rt(NPAIR) for _ in range(4))
        GU, SU = rt(NPAIR, dt=U32), rt(NPAIR, dt=U32)
        gc = [rt(1, dt=U32) for _ in range(2)]
        sc = [rt(1, dt=U32) for _ in range(2)]
        wc = [rt(1) for _ in range(2)]
        fnb = arr(0, D)
        fss = rt(2)
        assert at[0] <= 19 * SLAB

        @block.sync
        def _(sp):
            sp_passes = {-1: 0}
            for n, (t0, cnt) in enumerate(TILES):
                src = a["x"][0, t0 - META:t0 - META + cnt, :] if t0 else a["meta"]
                sp.dma_start(xtok[0:cnt, n, :], src).then_inc(s("ld_x"), 16)
            w_in = a["e_w_in"][0].rearrange("(p k) c -> p k c", k=KD)
            for g in range(11):
                if g >= 6:
                    sp.wait_ge(s("proj_done"), 2 * (g - 5))
                c0 = E_TILES[2 * g] * P
                sp.dma_start(wring[:, g % 6], w_in[:, :, c0:c0 + 2 * P]).then_inc(s(f"ld_w{g % 6}"), 16)
            sp.wait_ge(s("h_ready"), 5)
            sp.dma_start(wout, a["e_w_out"][0].rearrange("(k p) d -> p k d", p=P)).then_inc(s("ld_wout"), 16)

            def experts(y):
                p0 = sp_passes[y - 1]
                gate, up = (a[key][y].rearrange("e (p k) f -> p e (k f)", k=KD) for key in ("m_w_gate", "m_w_up"))
                down = a["m_w_down"][y].rearrange("e (p k) d -> p e (k d)", k=2)

                def pair(slot, i, uses):
                    sp.wait_ge(s(f"wfree{slot}"), uses)
                    sp.dma_start(slot_w[slot][:, :, 0:2048], gate[:, bass.ds(2 * i, 2), :]).then_inc(s(f"ld_gu{slot}"), 16)
                    sp.dma_start(slot_w[slot][:, :, 2048:4096], up[:, bass.ds(2 * i, 2), :]).then_inc(s(f"ld_gu{slot}"), 16)
                    sp.dma_start(slot_w[slot][:, :, 4096:6144], down[:, bass.ds(2 * i, 2), :]).then_inc(s(f"ld_d{slot}"), 16)

                with sp.Fori(0, NPAIR // 2) as n:
                    for slot in range(2):
                        pair(slot, 2 * n + slot, n + p0 * (NPAIR // 2) + 1 + y)
                sp.wait_ge(s("npass"), y + 1)
                passes = sp_passes[y] = sp.value_load(np_i[0:1, y:y + 1], min_val=1, max_val=5)
                with sp.If(passes > 1):
                    with sp.Fori(1, passes) as q:
                        with sp.Fori(0, NPAIR // 2) as n:
                            for slot in range(2):
                                pair(slot, 2 * n + slot, (q + p0) * (NPAIR // 2) + n + 1 + y)

            sp.wait_ge(s("proj_done"), 22)
            sp.sem_inc(s("wfree0"), 1)
            experts(0)
            if upto < 2:
                return
            sp.wait_ge(s("pe_end"), 1)
            w_o = a["o_w_in"][0].rearrange("(p k) c -> p k c", k=KD)
            for g, (c0, w) in enumerate(O_GROUPS):
                if g >= 6:
                    sp.wait_ge(s("o_grp"), g - 5)
                sp.dma_start(wring[:, g % 6, :, 0:w], w_o[:, :, c0:c0 + w]).then_inc(s(f"ld_w{g % 6}"), 16)
            sp.dma_start(wout, a["o_w_out"][0].rearrange("(k p) d -> p k d", p=P)).then_inc(s("ld_wout"), 16)
            sp.wait_ge(s("o_grp"), len(O_GROUPS))
            sp.sem_inc(s("wfree0"), 1)
            experts(1)
            sp.wait_ge(s("pe_end"), 2)
            sp.dma_start(fnb, a["final_norm"].rearrange("(o d) -> o d", o=1).broadcast_to([P, D])).then_inc(s("ld_fn"), 16)
            for n in range(2):
                sp.wait_ge(s("out_set"), n + 1)
                sp.dma_start(out[0, n * P:(n + 1) * P, :], yrow[:, n, 0, :]).then_inc(s("st_out"), 16)
            sp.wait_ge(s("st_out"), 32)

        @block.scalar
        def _(act):
            act_passes = {-1: 0}
            n_link = [0]

            def link(ins):
                n_link[0] += 1
                ins.then_inc(s("act_chain"), 1)
                act.wait_ge(s("act_chain"), n_link[0])

            for name, key in (("mu", "e_mu"), ("decay0", "e_decay0"), ("iclr0", "e_iclr0"), ("k_k", "e_k_k"),
                              ("k_a", "e_k_a"), ("r_k", "e_r_k"), ("ln_g", "e_ln_g"), ("ln_b", "e_ln_b"),
                              ("conv_b", "e_conv_b"), ("ba", "e_lru_ba"), ("bx", "e_lru_bx"), ("lam", "e_lru_lambda"),
                              ("g_b", "o_g_b"), ("gain", "o_head_gain")):
                rows = a[key].shape[1] // P
                act.dma_start(pvr[PV[name]:PV[name] + rows, :],
                              a[key].rearrange("o (r c) -> (o r) c", c=P)).then_inc(s("ld_pv"), 16)
            act.dma_start(pvr[PV["conv_w"]:PV["conv_w"] + 16, :],
                          a["e_conv_w"].rearrange("o i (r c) -> (o i r) c", c=P)).then_inc(s("ld_pv"), 16)
            for n, v in enumerate((a["e_norm"][0], a["o_norm"][0], a["m_norm"][0], a["m_norm"][1])):
                act.dma_start(gains[:, n, :], v.rearrange("(p k) -> p k", k=KD)).then_inc(s("ld_gain"), 16)
            act.dma_start(lora[0:64, :], a["e_decay_up"][0]).then_inc(s("ld_lora"), 16)
            act.dma_start(lora[64:128, :], a["e_iclr_up"][0]).then_inc(s("ld_lora"), 16)
            act.dma_start(gup, a["e_gate_up"][0]).then_inc(s("ld_lora"), 16)
            for n, key in enumerate(("e_lru_wa", "e_lru_wx")):
                for h in range(2):
                    act.dma_start(lruw[64 * h:64 * h + 64, n],
                                  a[key][0].rearrange("(j h) i o -> h i j o", h=2)[h]).then_inc(s("ld_lruw"), 16)
            act.wait_ge(s("h_ready"), 5)
            act.wait_ge(s("eps_set"), 1)
            for k in range(KD):
                nc.scalar.activation(sq[:, k], hT[:, k], ACT.Square).then_inc(s("sq0"), 1)
            act.wait_ge(s("aux_done"), 1)
            nc.scalar.activation(rs, ps[:, 4, 0:T], ACT.Sqrt, bias=epsb[:, 0:1], scale=1.0 / D).then_inc(s("aux_evac"), 1)
            act.wait_ge(s("lam_abs"), 1)
            nc.scalar.activation(slam[:, 1], slam[:, 0], ACT.Exp, scale=-1.0).then_inc(s("lam_exp"), 1)

            def evac(n):
                m = E_TILES[n]
                act.wait_ge(s("proj_done"), n + 1)
                src = ps[:, n % 4, 0:T]
                if 14 <= m < 18:
                    dst = xb[:, m - 14, 3:T + 3]
                elif m >= 18:
                    dst = gb[:, m - 18]
                else:
                    i = n - 8
                    if i == 0:
                        act.wait_ge(s("pads_zero"), 1)
                    if i >= 4:
                        act.wait_ge(s("shifted"), i - 3)
                    dst = raw[:, i % 4, 1:T + 1]
                nc.scalar.activation(dst, src, ACT.Copy).then_inc(s("proj_evac"), 1)

            def aux(u, *ins_of):
                act.wait_ge(s("aux_done"), u + 1)
                nc.scalar.activation(*ins_of[:3], **ins_of[3]).then_inc(s("aux_evac"), 1)

            for n in range(10):
                evac(n)
            for g in range(2):
                for j in range(4):
                    u = 1 + 4 * g + j
                    b = PV["ba" if g == 0 else "bx"] + j
                    aux(u, (ga, gi)[g][:, j], ps[:, 4 + u % 4, 0:T], ACT.Sigmoid, dict(bias=pv[:, b:b + 1]))
            act.wait_ge(s("shifted"), 2)
            nc.scalar.activation(WA[0:64, :], WA[0:64, :], ACT.Tanh).then_inc(s("lora_in"), 1)
            nc.scalar.activation(GD[:, :], GD[:, :], ACT.Sigmoid).then_inc(s("lora_in"), 1)
            for n in range(10, 14):
                evac(n)
            act.wait_ge(s("slam_set"), 1)
            act.wait_ge(s("aux_evac"), 9)
            for j in range(4):
                nc.scalar.activation(aa[:, j], ga[:, j], ACT.Exp, scale=slam[:, 5, j:j + 1]).then_inc(s("lru_a"), 1)
            for j in range(4):
                nc.scalar.activation(t1[:, j], ga[:, j], ACT.Tanh, scale=slam[:, 5, j:j + 1]).then_inc(s("lru_a"), 1)
            act.wait_ge(s("lru_in"), 1)
            nc.scalar.activation(t2, t2, ACT.Tanh, scale=0.7978845608028654).then_inc(s("lru_a"), 1)
            act.wait_ge(s("lru_in"), 2)
            nc.scalar.activation(t1, t1, ACT.Sqrt, scale=-1.0).then_inc(s("lru_a"), 1)
            act.wait_ge(s("pads_zero"), 1)
            for j in range(4):
                u = 9 + j
                aux(u, EX[:, j, PAD:TP], ps[:, 4 + u % 4, 0:T], ACT.Sigmoid,
                    dict(bias=pv[:, PV["decay0"] + j:PV["decay0"] + j + 1]))
            for j in range(4):
                u = 13 + j
                aux(u, aT[:, j, PAD:TP], ps[:, 4 + u % 4, 0:T], ACT.Sigmoid,
                    dict(bias=pv[:, PV["iclr0"] + j:PV["iclr0"] + j + 1]))
            for j in range(4):
                u = 17 + j
                act.wait_ge(s("aux_done"), 21)
                aux(u, GT[:, j, PAD:TP], ps[:, 4 + u % 4, 0:T], ACT.Copy, {})
            for n in range(14, 22):
                evac(n)
            for j in range(4):
                u = 21 + j
                aux(u, Kt[:, j], ps[:, 4 + u % 4, 0:TP], ACT.Sqrt, {})
            act.wait_ge(s("cum_set"), 1)
            nc.scalar.activation(EX, LW, ACT.Exp).then_inc(s("exps"), 1)
            act.wait_ge(s("ex_used"), 1)
            nc.scalar.activation(EX, CUM, ACT.Exp).then_inc(s("exps"), 1)
            act.wait_ge(s("ex_used"), 2)
            nc.scalar.activation(EX, CUM, ACT.Exp, scale=-1.0).then_inc(s("exps"), 1)
            for j in range(4):
                u = 25 + j
                aux(u, BV[:, j], ps[:, 4 + u % 4, 0:TP], ACT.Copy, {})
            for c in range(NC):
                act.wait_ge(s("pm_done"), c + 1)
                nc.scalar.activation(Vtk[:, c], ps[:, 2, 256:512].rearrange("p (j v) -> p j v", j=4), ACT.Copy)
                nc.scalar.activation(Ktk[:, c], ps[:, 3, 0:256].rearrange("p (j v) -> p j v", j=4), ACT.Copy)
                nc.scalar.activation(Btk[:, c], ps[:, 3, 256:512].rearrange("p (j v) -> p j v", j=4),
                                     ACT.Copy).then_inc(s("tok_evac"), 1)
            for n in range(5 * NC):
                act.wait_ge(s("y_done"), n + 1)
                nc.scalar.activation(YY[:, n % NC], ps[:, 4 + n % 2, 0:256].rearrange("p (j v) -> p j v", j=4),
                                     ACT.Copy).then_inc(s("y_evac"), 1)
            for c in range(NC):
                act.wait_ge(s("rh_done"), c + 1)
                nc.scalar.activation(RH, ps[:, 0, 0:256].rearrange("p (j v) -> p j v", j=4), ACT.Copy) \
                    .then_inc(s("rh_evac"), 1)
                act.wait_ge(s("sa_done"), c + 1)
                nc.scalar.activation(nSA, ps[:, 1, 0:256].rearrange("p (j v) -> p j v", j=4), ACT.Copy, scale=-1.0) \
                    .then_inc(s("sa_evac"), 1)
                act.wait_ge(s("o_done"), c + 1)
                nc.scalar.activation(oT[:, :, c * L:(c + 1) * L], ps[:, 2, 0:256].rearrange("p (j v) -> p j v", j=4),
                                     ACT.Copy).then_inc(s("o_evac"), 1)
            for j in range(4):
                u = 29 + j
                aux(u, LW[:, j, 0:T], ps[:, 4 + u % 4, 0:T], ACT.Copy, dict(scale=1.0 / L))
            for j in range(4):
                u = 33 + j
                aux(u, CUM[:, j, 0:T], ps[:, 4 + u % 4, 0:T], ACT.Sqrt, dict(bias=epsb[:, 1:2], scale=1.0 / L))

            def norm(i, dst, scratch, after):
                act.wait_ge(s(after[0]), after[1])
                for k in range(KD):
                    nc.scalar.activation(sq[:, k], hT[:, k], ACT.Square).then_inc(s("nsq"), 1)
                act.wait_ge(s("nss"), i)
                nc.scalar.activation(scratch, ps[:, 7, 0:T], ACT.Sqrt, bias=epsb[:, 0:1], scale=1.0 / D) \
                    .then_inc(s("nrs"), 1)

            def experts(y):
                p0 = act_passes[y - 1]
                norm(2 * y + 1, xnE, rsM, ("res_add", KD * (y + 1)))
                act.dma_start(wr[:, :, 0:NG], a["m_w_group"][y].rearrange("(p k) c -> p k c", k=KD)).then_inc(s("ld_wr"), 16)
                act.dma_start(wr[:, :, NG:], a["m_w_router"][y].rearrange("(p k) c -> p k c", k=KD)).then_inc(s("ld_wr"), 16)
                act.dma_start(BI[:, 0:NG], a["m_b_group"][y:y + 1, :].broadcast_to([P, NG])).then_inc(s("ld_bi"), 16)
                act.dma_start(BI[:, NG:], a["m_b_router"][y:y + 1, :].broadcast_to([P, NE])).then_inc(s("ld_bi"), 16)
                for n, (t0, cnt) in enumerate(TILES):
                    act.wait_ge(s("row_tr"), 3 * y + n + 1)
                    for hf in range(2):
                        ins = nc.scalar.activation(xrow[0:cnt, n, hf * 512:(hf + 1) * 512], ps[0:cnt, 2 * n + hf, :], ACT.Copy)
                    ins.then_inc(s("row_set"), 1)
                    act.wait_ge(s("row_set"), 3 * y + n + 1)
                    act.dma_start(xn_dram[t0:t0 + cnt, :], xrow[0:cnt, n, :]).then_inc(s("xn_st"), 16)
                act.wait_ge(s("route_in"), 2 * y + 1)
                nc.scalar.activation(eg, eg, ACT.Exp).then_inc(s("route_exp"), 1)
                act.wait_ge(s("route_in"), 2 * y + 2)
                nc.scalar.activation(w2, w2, ACT.Exp).then_inc(s("route_exp"), 1)
                act.wait_ge(s("npass"), y + 1)
                passes = act_passes[y] = act.value_load(np_i[0:1, y:y + 1], min_val=1, max_val=5)
                act.wait_ge(s("xn_st"), 48 * (y + 1))
                with act.Fori(0, passes) as q:
                    with act.Fori(0, NPAIR // 2) as n:
                        for b in range(2):
                            use = (q + p0) * (NPAIR // 2) + n
                            i = 2 * use + b
                            act.wait_ge(s("xt_done"), i + 1)
                            nc.scalar.activation(xgT[:, b, 0:4], ps[:, 0, :].rearrange("p (k t) -> p k t", k=4),
                                                 ACT.Copy).then_inc(s("xta"), 1)
                            act.wait_ge(s("gu_done"), i + 1)
                            nc.scalar.activation(sil, ps[:, 2, 0:FF], ACT.Silu).then_inc(s("sil"), 1)
                            act.wait_ge(s("ht_done"), i + 1)
                            nc.scalar.activation(hidT, ps[:, 3, 0:FF].rearrange("p (k t) -> p k t", k=2),
                                                 ACT.Copy).then_inc(s("hte"), 1)
                            act.wait_ge(s("rows_done"), i + 1)
                            act.wait_ge(s(f"idx_set{b}"), use + 1)
                            act.wait_ge(s(f"y_st{b}"), use * 16)
                            nc.scalar.activation(yst[:, b, 0:512], ps[:, 4, :], ACT.Copy, scale=wc[b]) \
                                .then_inc(s(f"ya{b}"), 1)
                act.wait_ge(s("scat"), y + 1)
                for n, (t0, cnt) in enumerate(TILES):
                    for x in range(2):
                        act.dma_start(yrow[0:cnt, n, x, :], y_dram[x * T + t0:x * T + t0 + cnt, :]) \
                            .then_inc(s(f"ld_y{n}"), 16)

            experts(0)
            if upto < 2:
                return
            act.dma_start(gupO[:, :], a["o_g_up"][0]).then_inc(s("ld_gupO"), 16)
            norm(2, xnO, rsO, ("h_ready", 10))
            for n in range(29):
                act.wait_ge(s("oproj"), n + 1)
                b = ps[:, n % 4]
                if n == 0:
                    args = (gdT, b[0:16, 0:T], ACT.Copy)
                elif n < 5:
                    args = (qO[:, n - 1, PAD:TP], b[:, 0:T], ACT.Copy)
                elif n < 9:
                    args = (kO[:, n - 5, PAD:TP], b[:, 0:T], ACT.Copy)
                elif n < 21:
                    g, t = (n - 9) // 3, (n - 9) % 3
                    rows = 64 if t == 2 else P
                    args = (Vo[0:rows, t, g * 256:(g + 1) * 256], b[0:rows, 0:256], ACT.Copy)
                else:
                    args = (rr[:, n - 21], b[:, 0:T], ACT.Silu)
                nc.scalar.activation(*args, **(dict(scale=float(P) ** -0.5) if 1 <= n < 5 else {})) \
                    .then_inc(s("oproj_evac"), 1)
                if n == 12:
                    act.wait_ge(s("opads"), 1)
                    for j in range(4):
                        act.wait_ge(s("gx"), j + 1)
                        b0 = PV["g_b"] + j
                        nc.scalar.activation(LA[:, j, PAD:TP], ps[:, 4 + j, 0:T], ACT.Identity, bias=pv[:, b0:b0 + 1]) \
                            .then_inc(s("gx_evac"), 1)
                    act.wait_ge(s("gx_evac"), 4)
                    link(nc.scalar.activation(EA[:, :, PAD:TP], LA[:, :, PAD:TP], ACT.Abs))
                    link(nc.scalar.activation(EA[:, :, PAD:TP], EA[:, :, PAD:TP], ACT.Exp, scale=-1.0))
                    nc.scalar.activation(EA[:, :, PAD:TP], EA[:, :, PAD:TP], ACT.Ln, bias=1.0).then_inc(s("gln"), 1)
            act.wait_ge(s("cu_set"), 1)
            nc.scalar.activation(EB, CU, ACT.Exp).then_inc(s("ge"), 1)
            act.wait_ge(s("kd_in"), 1)
            nc.scalar.activation(EA, EA, ACT.Exp).then_inc(s("ge"), 1)
            for i in range(6):
                act.wait_ge(s("lev_in"), i + 1)
                e = (EB, EA)[i % 2]
                nc.scalar.activation(e, e, ACT.Exp).then_inc(s("lev_e"), 1)
                if i == 0:
                    act.wait_ge(s("kdt_done"), 1)
                    for sl in range(3):
                        rows = 64 if sl == 2 else P
                        ins = nc.scalar.activation(kdt[0:rows, sl], ps[0:rows, 4 + sl, :].rearrange("p (h k) -> p h k", h=4),
                                                   ACT.Copy)
                    ins.then_inc(s("kdt_set"), 1)
            for i in range(NC):
                act.wait_ge(s("og_done"), i + 1)
                nc.scalar.activation(oG[:, :, i * L:(i + 1) * L], ps[:, i % 2, :].rearrange("p (x t) -> p x t", x=8),
                                     ACT.Copy).then_inc(s("og_evac"), 1)
            act.wait_ge(s("og_evac"), NC)
            for x in range(8):
                nc.scalar.activation(sqG[:, x], oG[:, x, PAD:TP], ACT.Square).then_inc(s("og_sq"), 1)
            for h in range(4):
                act.wait_ge(s("og_ss"), h + 1)
                nc.scalar.activation(LA[:, h, 0:T], ps[:, 4 + h, 0:T], ACT.Sqrt, bias=epsb[:, 0:1], scale=1.0 / 256) \
                    .then_inc(s("og_rs"), 1)
            experts(1)
            for n in range(2):
                act.wait_ge(s("fin_h"), n + 1)
                link(nc.scalar.activation(yrow[:, n, 1, :], yrow[:, n, 0, :], ACT.Square, accum_out=fss[:, n:n + 1]))
                nc.scalar.activation(fss[:, n:n + 1], fss[:, n:n + 1], ACT.Sqrt, bias=epsb[:, 0:1], scale=1.0 / D) \
                    .then_inc(s("fin_rs"), 1)

        @block.gpsimd
        def _(pool):
            pool_passes = {-1: 0}
            n_link = [0]

            def link(ins):
                n_link[0] += 1
                ins.then_inc(s("pool_chain"), 1)
                pool.wait_ge(s("pool_chain"), n_link[0])

            def keep(dst, src, pattern, base, mult=1, op=ALU.is_ge):
                link(pool.affine_select(out=dst, in_=src, pattern=pattern, compare_op=op, fill=0.0, base=base,
                                        channel_multiplier=mult))

            link(pool.memset(ones[:, :], 1.0))
            keep(ident[:, :], ones[:, :], [[-1, P]], 0, op=ALU.is_equal)
            keep(before[:, :], ones[:, :], [[1, P]], -1, mult=-1)
            pool.sem_inc(s("consts"), 1)
            link(pool.memset(onesbd[:, :], 0.0))
            for h in range(2):
                r = slice(64 * h, 64 * h + 64)
                link(pool.memset(onesbd[r, r], 1.0))
                keep(id64[r, :], ones[r, 0:64], [[-1, 64]], 0, op=ALU.is_equal)
                keep(m_ar[r, 0, :], ones[r, 0:64], [[1, L]], -1, mult=-1)
                keep(m_ar[r, 1, :], ones[r, 0:64], [[1, L]], 0, mult=-1)
                keep(m_n[r, :], ones[r, 0:64], [[-1, L]], -1)
            link(pool.memset(m_lev[:, :, :], 0.0))
            link(pool.memset(m_lev1n[:, :], 0.0))
            for h in range(2):
                r = slice(64 * h, 64 * h + 64)
                for lev in range(6):
                    m = 1 << lev
                    nb = L // (2 * m)
                    dst = m_lev[r, lev, :].rearrange("p (b x r) -> p b x r", x=2, r=m)[:, :, 1, :]
                    one = ones[r, 0:nb * m].rearrange("p (b r) -> p b r", r=m)
                    keep(dst, one, [[-2 * m, nb], [0, m]], 0)
                    keep(dst, dst, [[2 * m, nb], [0, m]], m - 1, mult=-1)
                dst = m_lev1n[r, :].rearrange("p (b x) -> p b x", x=2)[:, :, 0]
                keep(dst, ones[r, 0:32], [[-2, 32]], -1, op=ALU.is_equal)
            pool.iota(iota_i[:, :], [[1, SLOTS]], base=0, channel_multiplier=0)
            for n, (t0, _) in enumerate(TILES):
                link(pool.iota(tok_i[:, n:n + 1], [[1, 1]], base=t0, channel_multiplier=1))
            pool.sem_inc(s("consts"), 1)

            def experts(y):
                p0 = pool_passes[y - 1]
                pool.wait_ge(s("res_add"), KD * (y + 1))
                link(pool.memset(xg[:, :, :], 0.0))
                pool.wait_ge(s("npass"), y + 1)
                passes = pool_passes[y] = pool.value_load(np_i[0:1, y:y + 1], min_val=1, max_val=5)
                pool.wait_ge(s("xn_st"), 48 * (y + 1))
                last_row, last_out = pool.to_reg(T - 1), pool.to_reg(2 * T - 1)
                with pool.Fori(0, passes) as q:
                    with pool.Fori(0, NPAIR // 2) as n:
                        use = (q + p0) * (NPAIR // 2) + n
                        for b in range(2):
                            pool.wait_ge(s(f"idx_set{b}"), use + 1)
                            pool.wait_ge(s("xt_done"), 2 * use)
                            pool.sem_inc(s("pool_go"), 1)
                            pool.indirect_dma_start(out=xg[:, b, :], out_offset=None, in_=xn_dram,
                                                    in_offset=bass.IndirectOffsetOnAxis(ap=gc[b], axis=0),
                                                    bounds_check=last_row, oob_is_err=False).then_inc(s(f"xg_ld{b}"), 16)
                        for b in range(2):
                            pool.wait_ge(s(f"ya{b}"), use + 1)
                            pool.wait_ge(s(f"yd{b}"), use + 1)
                            pool.sem_inc(s("pool_go"), 1)
                            pool.indirect_dma_start(out=y_dram, out_offset=bass.IndirectOffsetOnAxis(ap=sc[b], axis=0),
                                                    in_=yst[:, b, :], in_offset=None,
                                                    bounds_check=last_out, oob_is_err=False).then_inc(s(f"y_st{b}"), 16)
                for b in range(2):
                    pool.wait_ge(s(f"y_st{b}"), (passes + p0) * (16 * NPAIR // 2))
                pool.nop()
                pool.sem_inc(s("scat"), 1)

            for y in range(2 if upto >= 2 else 1):
                experts(y)

        @block.tensor
        def _(pe):
            pe_passes = {-1: 0}
            pe.wait_ge(s("ld_x"), 48)
            pe.wait_ge(s("consts"), 1)
            for n, (t0, cnt) in enumerate(TILES):
                for k in range(KD):
                    b = 2 * n + k // 4 if n < 2 else 4
                    o = ps[:, b, (k % 4) * P:(k % 4) * P + cnt] if n < 2 else ps[:, b, k * META:(k + 1) * META]
                    ins = pe.transpose(o, xtok[0:cnt, n, k::KD], ident[0:cnt, 0:cnt])
                    if k % 4 == 3 and (n < 2 or k == 7):
                        ins.then_inc(s("h_tr"), 1)
            pe.wait_ge(s("ld_pv"), 240)
            pe.transpose(ps[:, 5, 0:NPV], pvr[0:NPV, :], ident[0:NPV, 0:NPV]).then_inc(s("pv_tr"), 1)
            pe.wait_ge(s("h_ready"), 5)
            for k in range(KD):
                pe.wait_ge(s("sq0"), k + 1)
                ins = pe.matmul(ps[:, 4, 0:T], ones[:, :], sq[:, k], start=(k == 0), stop=(k == KD - 1))
            ins.then_inc(s("aux_done"), 1)
            pe.wait_ge(s("pv_set"), 1)

            def proj(n):
                if n >= 4:
                    pe.wait_ge(s("proj_evac"), n - 3)
                if n % 2 == 0:
                    g = n // 2
                    pe.wait_ge(s(f"ld_w{g % 6}"), 16 * (g // 6 + 1))
                for k in range(KD):
                    if n == 0:
                        pe.wait_ge(s("xn0"), k + 1)
                    ins = pe.matmul(ps[:, n % 4, 0:T], wring[:, (n // 2) % 6, k, (n % 2) * P:(n % 2) * P + P],
                                    xnE[:, k], start=(k == 0), stop=(k == KD - 1))
                ins.then_inc(s("proj_done"), 1)

            def aux(u, *pairs, n=T):
                if u >= 5:
                    pe.wait_ge(s("aux_evac"), u - 3)
                for out_rows, lhs, rhs in pairs:
                    ins = pe.matmul(ps[out_rows, 4 + u % 4, 0:n], lhs, rhs, start=True, stop=True)
                ins.then_inc(s("aux_done"), 1)

            full = slice(0, P)
            for n in range(10):
                proj(n)
            pe.wait_ge(s("aux_evac"), 1)
            pe.wait_ge(s("conv"), 1)
            pe.wait_ge(s("ld_lruw"), 64)
            for g in range(2):
                for j in range(4):
                    aux(1 + 4 * g + j, *[(slice(64 * h, 64 * h + 64), lruw[64 * h:64 * h + 64, g, j],
                                          xc[64 * h:64 * h + 64, j]) for h in range(2)])
            for n in range(10, 14):
                proj(n)
            pe.wait_ge(s("ld_lora"), 48)
            pe.wait_ge(s("lora_in"), 2)
            for g in range(2):
                r = slice(64 * g, 64 * g + 64)
                for j in range(4):
                    aux(9 + 4 * g + j, (full, lora[r, j * P:(j + 1) * P], WA[r, :]))
            for j in range(4):
                aux(17 + j, (full, gup[:, j * P:(j + 1) * P], GD[:, :]))
            for n in range(14, 22):
                proj(n)
            pe.wait_ge(s("delta_in"), 1)
            pe.wait_ge(s("consts"), 2)
            for j in range(4):
                aux(21 + j, (full, onesbd[:, :], Bt[:, j]), n=TP)
            pe.wait_ge(s("delta_in"), 2)
            for j in range(4):
                aux(25 + j, (full, onesbd[:, :], KK[:, j]), n=TP)
            pe.wait_ge(s("delta_in"), 3)
            pe.wait_ge(s("aux_evac"), 29)
            for c in range(NC):
                t = slice(c * L, (c + 1) * L)
                if c >= 1:
                    pe.wait_ge(s("pm_evac"), c)
                    pe.wait_ge(s("tok_evac"), c)
                for j in range(4):
                    for h in range(2):
                        r = slice(64 * h, 64 * h + 64)
                        ar = AR[r, j, c].rearrange("p x t -> p (x t)")
                        pe.matmul(ps[r, 0, j * P:(j + 1) * P], Bt[r, j, t], ar, start=True, stop=True)
                        pe.matmul(ps[r, 1, j * P:(j + 1) * P], Kt[r, j, t], ar, start=True, stop=True)
                        pe.matmul(ps[r, 5, j * L:(j + 1) * L], AR[r, j, c, 0], Bt[r, j, t], start=True, stop=True)
                        pe.matmul(ps[r, 2, 256 + j * L:256 + (j + 1) * L], vT[r, j, t], id64[r, :], start=True, stop=True)
                        pe.matmul(ps[r, 3, j * L:(j + 1) * L], Kt[r, j, t], id64[r, :], start=True, stop=True)
                        ins = pe.matmul(ps[r, 3, 256 + j * L:256 + (j + 1) * L], Bt[r, j, t], id64[r, :],
                                        start=True, stop=True)
                ins.then_inc(s("pm_done"), 1)
            pe.wait_ge(s("pm_evac"), NC)
            for n in range(5 * NC):
                c = n % NC
                pe.wait_ge(s("x_set"), n + 1)
                if n >= 2:
                    pe.wait_ge(s("y_evac"), n - 1)
                for j in range(4):
                    for h in range(2):
                        r = slice(64 * h, 64 * h + 64)
                        ins = pe.matmul(ps[r, 4 + n % 2, j * L:(j + 1) * L], CT[r, c, j], X[r, c, j],
                                        start=True, stop=True)
                ins.then_inc(s("y_done"), 1)
                pe.wait_ge(s("y_evac"), n + 1)
                if n >= 2:
                    pe.wait_ge(s("z_used"), n - 1)
                for j in range(4):
                    for h in range(2):
                        r = slice(64 * h, 64 * h + 64)
                        pe.matmul(ps[r, 6 + n % 2, j * L:(j + 1) * L], XT[r, c, j], YY[r, c, j], start=True, stop=True)
                        ins = pe.matmul(ps[r, 6 + n % 2, 256 + j * L:256 + (j + 1) * L], YY[r, c, j], XT[r, c, j],
                                        start=True, stop=True)
                ins.then_inc(s("z_done"), 1)
            pe.wait_ge(s("z_used"), 5 * NC)
            pe.wait_ge(s("pm_evac"), NC)
            pe.wait_ge(s("tok_evac"), NC)
            for c in range(NC):
                t = slice(c * L, (c + 1) * L)
                pe.wait_ge(s("st_set"), c + 1)

                def heads(bank, *terms):
                    for j in range(4):
                        for i, (lhs, rhs) in enumerate(terms):
                            for h in range(2):
                                r = slice(64 * h, 64 * h + 64)
                                ins = pe.matmul(ps[r, bank, j * L:(j + 1) * L], lhs(r, j), rhs(r, j),
                                                start=(i == 0), stop=(i == len(terms) - 1))
                    return ins

                heads(0, (lambda r, j: AR[r, j, c, 0], lambda r, j: ST[r, j]),
                      (lambda r, j: MB[r, c, j, 0], lambda r, j: Vtk[r, c, j])).then_inc(s("rh_done"), 1)
                pe.wait_ge(s("rh_evac"), c + 1)
                heads(1, (lambda r, j: XT[r, c, j], lambda r, j: RH[r, j])).then_inc(s("sa_done"), 1)
                pe.wait_ge(s("sa_evac"), c + 1)
                heads(3, (lambda r, j: Ktk[r, c, j], lambda r, j: Vtk[r, c, j]),
                      (lambda r, j: Btk[r, c, j], lambda r, j: nSA[r, j])).then_inc(s("ds_done"), 1)
                if c >= 1:
                    pe.wait_ge(s("o_evac"), c)
                heads(2, (lambda r, j: ST[r, j], lambda r, j: AR[r, j, c, 1]),
                      (lambda r, j: Vtk[r, c, j], lambda r, j: MB[r, c, j, 1]),
                      (lambda r, j: nSA[r, j], lambda r, j: MA[r, c, j, 1])).then_inc(s("o_done"), 1)
            pe.wait_ge(s("o_evac"), NC)
            for j in range(4):
                aux(29 + j, (full, onesbd[:, :], oT[:, j, PAD:TP]))
            for j in range(4):
                pe.wait_ge(s("o_sq"), j + 1)
                aux(33 + j, (full, onesbd[:, :], X.rearrange("p c j t -> p (c j t)").rearrange(
                    "p (j t) -> p j t", j=4)[:, j, PAD:TP]))

            def out_proj(y):
                pe.wait_ge(s("ld_wout"), 16 * (y + 1))
                pe.wait_ge(s("mix_ready"), y + 1)
                for m in range(KD):
                    if m >= 4:
                        pe.wait_ge(s("res_add"), KD * y + m - 3)
                    for k in range(8):
                        ins = pe.matmul(ps[:, m % 4, 0:T], wout[:, k, m::KD], mixT[:, k], start=(k == 0), stop=(k == 7))
                    ins.then_inc(s("res_done"), 1)

            def norm(i):
                for k in range(KD):
                    pe.wait_ge(s("nsq"), 8 * i + k - 7)
                    ins = pe.matmul(ps[:, 7, 0:T], ones[:, :], sq[:, k], start=(k == 0), stop=(k == KD - 1))
                ins.then_inc(s("nss"), 1)

            def experts(y):
                p0 = pe_passes[y - 1]
                norm(2 * y + 1)
                pe.wait_ge(s("xn"), KD * (2 * y + 1))
                pe.wait_ge(s("ld_wr"), 32 * (y + 1))
                for n, (t0, cnt) in enumerate(TILES):
                    for k in range(KD):
                        ins = pe.matmul(ps[0:cnt, 6, n * 36:n * 36 + 36], xnE[:, k, t0:t0 + cnt], wr[:, k, :],
                                        start=(k == 0), stop=(k == KD - 1))
                ins.then_inc(s("lg_done"), 1)
                for n, (t0, cnt) in enumerate(TILES):
                    for k in range(KD):
                        ins = pe.transpose(ps[0:cnt, 2 * n + k // 4, (k % 4) * P:(k % 4) * P + P],
                                           xnE[:, k, t0:t0 + cnt], ident[:, :])
                    ins.then_inc(s("row_tr"), 1)
                pe.wait_ge(s("A_set"), y + 1)
                M = META
                terms = [[(before[:, :], AA[:, 0])],
                         [(ones[:, :], AA[:, 0]), (before[:, :], AA[:, 1])],
                         [(ones[:, :], AA[:, 0]), (ones[:, :], AA[:, 1]), (before[0:M, :], AA[0:M, 2])],
                         [(ones[:, :], AA[:, 0]), (ones[:, :], AA[:, 1]), (ones[0:M, :], AA[0:M, 2])]]
                for n, t in enumerate(terms):
                    for i, (lhs, rhs) in enumerate(t):
                        ins = pe.matmul(ps[:, 7, n * NE:(n + 1) * NE], lhs, rhs, start=(i == 0), stop=(i == len(t) - 1))
                ins.then_inc(s("rk_done"), 1)
                pe.wait_ge(s("npass"), y + 1)
                passes = pe_passes[y] = pe.value_load(np_i[0:1, y:y + 1], min_val=1, max_val=5)
                pe.wait_ge(s("row_set"), 3 * y + 3)
                with pe.Fori(0, passes) as q:
                    pe.wait_ge(s("R_set"), q + p0 + 1)
                    for i in range(NPAIR):
                        for n, (_, cnt) in enumerate(TILES):
                            ins = pe.matmul(ps[:, 6, i * 6:i * 6 + 6], R[0:cnt, n, 2 * i:2 * i + 2, :].rearrange(
                                "p e c -> p (e c)"), VV[0:cnt, n, i, :], start=(n == 0), stop=(n == 2))
                    ins.then_inc(s("tb_done"), 1)
                    with pe.Fori(0, NPAIR // 2) as n:
                        for b in range(2):
                            use = (q + p0) * (NPAIR // 2) + n
                            i = 2 * use + b
                            w = slot_w[b]
                            pe.wait_ge(s(f"xg_ld{b}"), use * 16 + 16)
                            pe.wait_ge(s("xta"), i)
                            pe.wait_ge(s("xtd"), i)
                            for k in range(KD):
                                ins = pe.transpose(ps[:, k // 4, (k % 4) * P:(k % 4) * P + P],
                                                   xg[:, b, k * P:(k + 1) * P], ident[:, :])
                            ins.then_inc(s("xt_done"), 1)
                            pe.wait_ge(s("xta"), i + 1)
                            pe.wait_ge(s("xtd"), i + 1)
                            pe.wait_ge(s(f"ld_gu{b}"), use * 32 + 32)
                            pe.wait_ge(s("hid"), i)
                            for k in range(KD):
                                for e in range(2):
                                    r = slice(64 * e, 64 * e + 64)
                                    gu = w[:, e, 0:4096].rearrange("p (x k f) -> p x k f", x=2, k=KD)
                                    ins = pe.matmul(ps[r, 2, :], xgT[:, b, k, r], gu[:, :, k, :],
                                                    start=(k == 0), stop=(k == KD - 1))
                            ins.then_inc(s("gu_done"), 1)
                            pe.wait_ge(s("hid"), i + 1)
                            pe.wait_ge(s("hte"), i)
                            for k in range(2):
                                ins = pe.transpose(ps[:, 3, k * P:(k + 1) * P], hid[:, k::2], ident[:, :])
                            ins.then_inc(s("ht_done"), 1)
                            pe.wait_ge(s("hte"), i + 1)
                            pe.wait_ge(s(f"ld_d{b}"), use * 16 + 16)
                            if b == 0:
                                pe.wait_ge(s("ya1"), use)
                                pe.wait_ge(s("yd1"), use)
                            else:
                                pe.wait_ge(s("ya0"), use + 1)
                                pe.wait_ge(s("yd0"), use + 1)
                            for hf in range(2):
                                for k in range(2):
                                    for e in range(2):
                                        r = slice(64 * e, 64 * e + 64)
                                        dn = w[:, e, 4096 + k * D + hf * 512:4096 + k * D + hf * 512 + 512]
                                        ins = pe.matmul(ps[r, 4 + hf, :], hidT[:, k, r], dn, start=(k == 0), stop=(k == 1))
                            ins.then_inc(s("rows_done"), 1)
                            pe.wait_ge(s("rows_done"), i + 1)
                            pe.sem_inc(s(f"wfree{b}"), 1)
                pe.sem_inc(s("pe_end"), 1)
                if y == 0:
                    for n, (t0, cnt) in enumerate(TILES):
                        pe.wait_ge(s("y_sum"), n + 1)
                        for k in range(KD):
                            bk = 2 * n + k // 4 if n < 2 else 4
                            o = ps[:, bk, (k % 4) * P:(k % 4) * P + cnt] if n < 2 else ps[:, bk, k * META:(k + 1) * META]
                            ins = pe.transpose(o, yrow[0:cnt, n, 0, k::KD], ident[0:cnt, 0:cnt])
                            if k % 4 == 3 and (n < 2 or k == 7):
                                ins.then_inc(s("h_tr"), 1)
                else:
                    pe.wait_ge(s("y_sum"), 4)
                    for n, (t0, cnt) in enumerate(TILES[:2]):
                        for k in range(KD):
                            ins = pe.transpose(ps[:, 2 * n + k // 4, (k % 4) * P:(k % 4) * P + P],
                                               hT[:, k, t0:t0 + P], ident[:, :])
                        ins.then_inc(s("hr_done"), 1)

            out_proj(0)
            experts(0)
            if upto < 2:
                return
            norm(2)
            pe.wait_ge(s("ld_gupO"), 16)
            pe.wait_ge(s("xn"), 2 * KD)
            unit = 0
            for g, (c0, w) in enumerate(O_GROUPS):
                pe.wait_ge(s(f"ld_w{g % 6}"), 16 * (g // 6 + 1 + (2 if g % 6 < 5 else 1)))
                wg = wring[:, g % 6]
                if g == 0:
                    todo = [(slice(0, 16), T, lambda k: wg[:, k, 0:16], lambda k: xnO[:, k, PAD:TP])]
                elif 5 <= g < 9:
                    todo = [(slice(0, cnt), 256, lambda k, c=c0_, n=cnt: xnO[:, k, c:c + n], lambda k: wg[:, k, :])
                            for c0_, cnt in ((L, P), (3 * L, P), (0, L))]
                else:
                    todo = [(slice(0, P), T, lambda k, m=m: wg[:, k, m * P:(m + 1) * P], lambda k: xnO[:, k, PAD:TP])
                            for m in range(2)]
                for j, (rows, n, lhs, rhs) in enumerate(todo):
                    if unit >= 4:
                        pe.wait_ge(s("oproj_evac"), unit - 3)
                    for k in range(KD):
                        ins = pe.matmul(ps[rows, unit % 4, 0:n], lhs(k), rhs(k), start=(k == 0), stop=(k == KD - 1))
                    ins.then_inc(s("oproj"), 1)
                    unit += 1
                    if j == len(todo) - 1:
                        pe.wait_ge(s("oproj"), unit)
                        pe.sem_inc(s("o_grp"), 1)
                if g == 4:
                    for j in range(4):
                        pe.matmul(ps[:, 4 + j, 0:T], gupO[:, j * P:(j + 1) * P], gdT, start=True, stop=True) \
                            .then_inc(s("gx"), 1)
            pe.wait_ge(s("kd_set"), 1)
            pe.wait_ge(s("gx_evac"), 4)
            for h in range(4):
                for c in range(NC):
                    sl, half = PLACE[c]
                    ins = pe.matmul(ps[64 * half:64 * half + 64, 4 + sl, h * P:(h + 1) * P], KDc[:, h, c * L:(c + 1) * L],
                                    ident[:, :], start=True, stop=True)
            ins.then_inc(s("kdt_done"), 1)
            pe.wait_ge(s("oproj_evac"), 29)
            for i in range(7):
                if i > 0:
                    pe.wait_ge(s("qk_set"), i)
                if i >= 2:
                    pe.wait_ge(s("pt_used"), i - 1)
                qq, kk = (qO, kO) if i == 0 else (QH, KH)
                for h in range(4):
                    for c in (1, 2, 3, 4, 0):
                        sl, half = PLACE[c]
                        bk, o = (2 * (i % 2), sl * 256) if sl < 2 else (2 * (i % 2) + 1, 0)
                        ins = pe.matmul(ps[64 * half:64 * half + 64, bk, o + h * L:o + (h + 1) * L],
                                        kk[:, h, c * L:(c + 1) * L], qq[:, h, c * L:(c + 1) * L], start=True, stop=True)
                ins.then_inc(s("pt_done"), 1)
            pe.wait_ge(s("pt_used"), 7)
            pe.wait_ge(s("kdt_set"), 1)
            for c in range(NC):
                sl, half = PLACE[c]
                r = slice(64 * half, 64 * half + 64)
                pe.wait_ge(s("sg_set"), 4 * c + 1)
                if c >= 1:
                    pe.wait_ge(s("sg_set"), 4 * c + 1)
                if c >= 2:
                    pe.wait_ge(s("og_evac"), c - 1)
                for h in range(4):
                    for x in range(2):
                        o = ps[:, c % 2, (2 * h + x) * L:(2 * h + x + 1) * L]
                        v0 = h * 256 + x * P
                        pe.matmul(o, SG[:, h, x * P:(x + 1) * P], QE[:, h, c * L:(c + 1) * L], start=True, stop=False)
                        ins = pe.matmul(o, Vo[r, sl, v0:v0 + P], PT[r, sl, h, :], start=False, stop=True)
                ins.then_inc(s("og_done"), 1)
                if c < NC - 1:
                    for h in range(4):
                        ins = pe.matmul(ps[:, 2 + h // 2, (h % 2) * 256:(h % 2) * 256 + 256], kdt[r, sl, h, :],
                                        Vo[r, sl, h * 256:(h + 1) * 256], start=True, stop=True)
                    ins.then_inc(s("sg_done"), 1)
            for h in range(4):
                for x in range(2):
                    pe.wait_ge(s("og_sq"), 2 * h + x + 1)
                    ins = pe.matmul(ps[:, 4 + h, 0:T], ones[:, :], sqG[:, 2 * h + x], start=(x == 0), stop=(x == 1))
                ins.then_inc(s("og_ss"), 1)
            out_proj(1)
            experts(1)

        @block.vector
        def _(v):
            v_passes = {-1: 0}
            n_link = [0]

            def link(ins):
                n_link[0] += 1
                ins.then_inc(s("dve_chain"), 1)
                v.wait_ge(s("dve_chain"), n_link[0])

            def col(name, j):
                return pv[:, PV[name] + j:PV[name] + j + 1]

            tt = v.tensor_tensor
            stt = v.scalar_tensor_tensor
            v.memset(epsb[:, 0:1], EPS)
            v.memset(epsb[:, 1:2], GN_EPS).then_inc(s("eps_set"), 1)
            for i in range(5):
                v.wait_ge(s("h_tr"), i + 1)
                if i < 4:
                    t0 = TILES[i // 2][0]
                    k0 = 4 * (i % 2)
                    v.tensor_copy(hT[:, k0:k0 + 4, t0:t0 + P], ps[:, i, :].rearrange("p (k t) -> p k t", k=4)) \
                        .then_inc(s("h_ready"), 1)
                else:
                    v.tensor_copy(hT[:, :, 0:META], ps[:, 4, 0:P].rearrange("p (k t) -> p k t", k=8)) \
                        .then_inc(s("h_ready"), 1)
            v.wait_ge(s("pv_tr"), 1)
            v.tensor_copy(pv[:, :], ps[:, 5, 0:NPV]).then_inc(s("pv_set"), 1)
            v.wait_ge(s("pv_set"), 1)
            lam = pv[:, PV["lam"]:PV["lam"] + 4]
            link(v.tensor_scalar(slam[:, 2], lam, -1.0, None, ALU.mult))
            tt(slam[:, 0], lam, slam[:, 2], ALU.max).then_inc(s("lam_abs"), 1)
            link(v.tensor_scalar(omka[:, :], pv[:, PV["k_a"]:PV["k_a"] + 4], -1.0, 1.0, ALU.mult, ALU.add))
            v.wait_ge(s("aux_evac"), 1)
            v.wait_ge(s("ld_gain"), 64)
            link(v.reciprocal(rs, rs))
            for k in range(KD):
                stt(out=xnE[:, k], in0=hT[:, k], scalar=gains[:, 0, k:k + 1], in1=rs, op0=ALU.mult, op1=ALU.mult) \
                    .then_inc(s("xn0"), 1)
            v.wait_ge(s("xn0"), KD)
            v.memset(xb[:, :, 0:3], 0.0)
            v.memset(raw[:, :, 0:1], 0.0)
            for x in (rT, kT, vT, aT, EX):
                if x is not EX:
                    v.memset(x[:, :, 0:PAD], 0.0)
            v.memset(reset[:, :], 1.0)
            link(v.memset(EX[:, :, 0:PAD], 0.0))
            link(v.memset(reset[:, :].rearrange("p (c t) -> p c t", t=L)[:, :, 0], 0.0))
            v.sem_inc(s("pads_zero"), 1)
            v.wait_ge(s("lam_exp"), 1)
            link(v.tensor_scalar(slam[:, 3], slam[:, 1], 2.0, None, ALU.add))
            link(v.reciprocal(slam[:, 3], slam[:, 3]))
            link(tt(slam[:, 3], slam[:, 3], slam[:, 1], ALU.mult))
            link(tt(slam[:, 4], slam[:, 3], slam[:, 3], ALU.mult))
            link(v.memset(slam[:, 5], 1.0 / 17))
            for i in range(7, -1, -1):
                link(tt(slam[:, 5], slam[:, 5], slam[:, 4], ALU.mult))
                link(v.tensor_scalar(slam[:, 5], slam[:, 5], 1.0 / (2 * i + 1), None, ALU.add))
            link(tt(slam[:, 5], slam[:, 5], slam[:, 3], ALU.mult))
            link(v.tensor_scalar(slam[:, 2], slam[:, 2], 0.0, None, ALU.max))
            link(stt(out=slam[:, 5], in0=slam[:, 5], scalar=2.0, in1=slam[:, 2], op0=ALU.mult, op1=ALU.add))
            v.tensor_scalar(slam[:, 5], slam[:, 5], -8.0, None, ALU.mult).then_inc(s("slam_set"), 1)
            v.wait_ge(s("proj_evac"), 4)
            for j in range(4):
                cw = [pv[:, PV["conv_w"] + 4 * i + j:PV["conv_w"] + 4 * i + j + 1] for i in range(4)]
                link(v.tensor_scalar(xc[:, j], xb[:, j, 3:T + 3], cw[3], col("conv_b", j), ALU.mult, ALU.add))
                for i in range(3):
                    link(stt(out=xc[:, j], in0=xb[:, j, i:i + T], scalar=cw[i], in1=xc[:, j], op0=ALU.mult, op1=ALU.add))
            v.sem_inc(s("conv"), 1)
            v.wait_ge(s("proj_evac"), 8)
            link(tt(t2, gb, gb, ALU.mult))
            link(v.tensor_scalar(t2, t2, 0.044715, 1.0, ALU.mult, ALU.add))
            tt(t2, t2, gb, ALU.mult).then_inc(s("lru_in"), 1)

            def shift(i, dst, m):
                v.wait_ge(s("proj_evac"), 9 + i)
                q = raw[:, i % 4]
                link(tt(DT, q[:, 0:T], q[:, 1:T + 1], ALU.subtract))
                stt(out=dst, in0=DT, scalar=col("mu", m), in1=q[:, 1:T + 1], op0=ALU.mult, op1=ALU.add) \
                    .then_inc(s("shifted"), 1)
                v.wait_ge(s("shifted"), i + 1)

            shift(0, WA, 12)
            shift(1, GD, 13)
            for j in range(4):
                shift(2 + j, kT[:, j, PAD:TP], 4 + j)
            v.wait_ge(s("lru_a"), 8)
            link(tt(xb[:, :, 0:T], aa, aa, ALU.mult))
            stt(out=t1, in0=xb[:, :, 0:T], scalar=1.0, in1=t1, op0=ALU.add, op1=ALU.mult).then_inc(s("lru_in"), 1)
            v.wait_ge(s("lru_a"), 9)
            link(stt(out=t2, in0=t2, scalar=1.0, in1=gb, op0=ALU.add, op1=ALU.mult))
            link(tt(gi, gi, xc, ALU.mult))
            v.wait_ge(s("lru_a"), 10)
            link(tt(gi, gi, t1, ALU.mult))
            for j in range(4):
                last = v.tensor_tensor_scan(hh[:, j], aa[:, j], gi[:, j], 0.0, ALU.mult, ALU.add)
            link(last)
            link(stt(out=mixT[:, 4:8], in0=hh, scalar=0.5, in1=t2, op0=ALU.mult, op1=ALU.mult))
            for j in range(4):
                shift(6 + j, rT[:, j, PAD:TP], j)
            for j in range(4):
                shift(10 + j, vT[:, j, PAD:TP], 8 + j)
            for j in range(4):
                last = v.tensor_scalar(KK[:, j], kT[:, j], col("k_k", j), None, ALU.mult)
            link(last)
            tt(Bt, KK, KK, ALU.mult).then_inc(s("delta_in"), 1)
            v.wait_ge(s("aux_evac"), 17)
            link(v.tensor_scalar(LW, EX, -0.6065306597126334, None, ALU.mult))
            link(v.tensor_tensor_scan(CUM.rearrange("p j t -> p (j t)"), reset[:, :], LW.rearrange("p j t -> p (j t)"),
                                      0.0, ALU.mult, ALU.add))
            tt(LW, CUM, LW, ALU.subtract).then_inc(s("cum_set"), 1)
            v.wait_ge(s("aux_evac"), 25)
            link(v.tensor_scalar(Kt, Kt, 1e-12, None, ALU.max))
            link(v.reciprocal(Kt, Kt))
            link(tt(KK, KK, Kt, ALU.mult))
            for j in range(4):
                last = v.tensor_scalar(KM[:, j], aT[:, j], col("k_a", j), omka[:, j:j + 1], ALU.mult, ALU.add)
            link(last)
            link(tt(KM, KM, kT, ALU.mult))
            link(tt(Bt, KK, aT, ALU.mult))
            ar = AR.rearrange("p j c x t -> p (j c) x t")

            def ch(x):
                return x.rearrange("p j (c t) -> p (j c) t", t=L)

            v.wait_ge(s("exps"), 1)
            tt(ar[:, :, 0], ch(KK), ch(EX), ALU.mult).then_inc(s("ex_used"), 1)
            v.wait_ge(s("ex_used"), 1)
            for j in range(4):
                last = stt(out=KK[:, j], in0=rT[:, j], scalar=col("r_k", j), in1=KM[:, j], op0=ALU.mult, op1=ALU.mult)
            last.then_inc(s("delta_in"), 1)
            v.wait_ge(s("exps"), 2)
            v.tensor_copy(dlast[:, :, :], EX.rearrange("p j (c t) -> p j c t", t=L)[:, :, :, L - 1])
            tt(ar[:, :, 1], ch(rT), ch(EX), ALU.mult).then_inc(s("ex_used"), 1)
            v.wait_ge(s("exps"), 3)
            tt(Kt, KM, EX, ALU.mult)
            tt(Bt, Bt, EX, ALU.mult).then_inc(s("delta_in"), 1)
            v.wait_ge(s("aux_evac"), 29)
            link(tt(BV, BV, vT, ALU.mult))
            def over(m, n):
                return m[:, None, :].to_broadcast([P, n, m.shape[-1]]) if len(m.shape) == 2 else None

            v.wait_ge(s("consts"), 2)
            for c in range(NC):
                v.wait_ge(s("pm_done"), c + 1)
                mar = m_ar[:, :, :].rearrange("p x t -> p (x t)").unsqueeze(1).to_broadcast([P, 4, 2 * L])
                tt(MA[:, c].rearrange("p j x t -> p j (x t)"), ps[:, 0, :].rearrange("p (j y) -> p j y", j=4), mar, ALU.mult)
                tt(MB[:, c].rearrange("p j x t -> p j (x t)"), ps[:, 1, :].rearrange("p (j y) -> p j y", j=4), mar, ALU.mult)
                tt(NN[:, c], ps[:, 5, 0:256].rearrange("p (j y) -> p j y", j=4),
                   m_n[:, :].unsqueeze(1).to_broadcast([P, 4, L]), ALU.mult).then_inc(s("pm_evac"), 1)
            v.wait_ge(s("pm_evac"), NC)
            nn = NN.rearrange("p c j t -> p (c j) t")
            nt = MA.rearrange("p c j x t -> p (c j) x t")[:, :, 0]
            xx, xt = X.rearrange("p c j t -> p (c j) t"), XT.rearrange("p c j t -> p (c j) t")

            def wide(m):
                return m.unsqueeze(1).to_broadcast([P, 4 * NC, L])

            v.tensor_tensor(xx, nn, wide(m_lev1n[:, :]), ALU.mult)
            link(v.tensor_tensor(xt, nt, wide(m_lev[:, 0]), ALU.mult))
            tt(xx, wide(id64[:, :]), xx, ALU.subtract)
            link(tt(xt, wide(id64[:, :]), xt, ALU.subtract))
            for n in range(5 * NC):
                lev, c = n // NC + 1, n % NC
                tt(CT[:, c], MA[:, c, :, 0], m_lev[:, lev].unsqueeze(1).to_broadcast([P, 4, L]), ALU.mult) \
                    .then_inc(s("x_set"), 1) if lev == 1 else None
            for n in range(5 * NC):
                lev, c = n // NC + 1, n % NC
                v.wait_ge(s("z_done"), n + 1)
                z = ps[:, 6 + n % 2, :].rearrange("p (x j t) -> p x j t", x=2, j=4)
                tt(X[:, c], X[:, c], z[:, 0], ALU.subtract)
                if lev < 5:
                    tt(CT[:, c], MA[:, c, :, 0], m_lev[:, lev + 1].unsqueeze(1).to_broadcast([P, 4, L]), ALU.mult) \
                        .then_inc(s("x_pre"), 1)
                tt(XT[:, c], XT[:, c], z[:, 1], ALU.subtract).then_inc(s("z_used"), 1)
                if lev < 5:
                    v.wait_ge(s("z_used"), n + 1)
                    v.sem_inc(s("x_set"), 1)
            v.wait_ge(s("pm_done"), NC)
            v.memset(ST, 0.0).then_inc(s("st_set"), 1)
            for c in range(NC):
                v.wait_ge(s("ds_done"), c + 1)
                v.wait_ge(s("st_set"), c + 1)
                link(tt(STn, ST, ps[:, 3, 0:256].rearrange("p (j v) -> p j v", j=4), ALU.add))
                v.wait_ge(s("o_done"), c + 1)
                tt(ST, STn, dlast[:, :, c:c + 1].to_broadcast([P, 4, L]), ALU.mult).then_inc(s("st_set"), 1)
            oq = X.rearrange("p c j t -> p (c j t)").rearrange("p (j t) -> p j t", j=4)
            mean, root = LW, CUM
            for j in range(4):
                v.wait_ge(s("aux_evac"), 30 + j)
                v.wait_ge(s("o_evac"), NC)
                link(tt(oT[:, j, PAD:TP], oT[:, j, PAD:TP], mean[:, j, 0:T], ALU.subtract))
                tt(oq[:, j, PAD:TP], oT[:, j, PAD:TP], oT[:, j, PAD:TP], ALU.mult).then_inc(s("o_sq"), 1)
            for j in range(4):
                v.wait_ge(s("aux_evac"), 34 + j)
                link(v.reciprocal(root[:, j, 0:T], root[:, j, 0:T]))
                link(tt(oT[:, j, PAD:TP], oT[:, j, PAD:TP], root[:, j, 0:T], ALU.mult))
                link(v.tensor_scalar(oT[:, j, PAD:TP], oT[:, j, PAD:TP], col("ln_g", j), col("ln_b", j), ALU.mult, ALU.add))
                link(tt(oT[:, j, PAD:TP], oT[:, j, PAD:TP], BV[:, j, PAD:TP], ALU.add))
                ins = tt(mixT[:, j], oT[:, j, PAD:TP], GT[:, j, PAD:TP], ALU.mult)
            ins.then_inc(s("mix_ready"), 1)

            def res_add(y):
                for m in range(KD):
                    v.wait_ge(s("res_done"), KD * y + m + 1)
                    tt(hT[:, m], hT[:, m], ps[:, m % 4, 0:T], ALU.add).then_inc(s("res_add"), 1)
                v.wait_ge(s("res_add"), KD * (y + 1))
                v.sem_inc(s("wfree1"), 1)

            def norm(i, gain, scratch, dst):
                v.wait_ge(s("nrs"), i)
                link(v.reciprocal(scratch, scratch))
                for k in range(KD):
                    stt(out=dst[:, k], in0=hT[:, k], scalar=gains[:, gain, k:k + 1], in1=scratch,
                        op0=ALU.mult, op1=ALU.mult).then_inc(s("xn"), 1)

            def wide3(x, n):
                return x.unsqueeze(2).to_broadcast([P, 3, n])

            def first_max(dst, src, top, n, tmp):
                link(tt(tmp, src, wide3(top, n), ALU.is_equal))
                for i in range(n):
                    ins = v.tensor_scalar(tmp[:, :, i], tmp[:, :, i], float(n - i), None, ALU.mult)
                link(ins)
                link(v.tensor_reduce(gsum, tmp, AXX, ALU.max))
                link(tt(dst, tmp, wide3(gsum, n), ALU.is_equal))

            def experts(y):
                p0 = v_passes[y - 1]
                norm(2 * y + 1, 2 + y, rsM, xnE)
                v.wait_ge(s("lg_done"), y + 1)
                v.wait_ge(s("ld_bi"), 32 * (y + 1))
                link(v.memset(LG, 0.0))
                for n, (_, cnt) in enumerate(TILES):
                    ins = tt(LG[0:cnt, n], ps[0:cnt, 6, n * 36:n * 36 + 36], BI[0:cnt], ALU.add)
                link(ins)
                link(v.tensor_reduce(gmax, LG[:, :, 0:NG], AXX, ALU.max))
                tt(eg, LG[:, :, 0:NG], wide3(gmax, NG), ALU.subtract).then_inc(s("route_in"), 1)
                first_max(ohg, LG[:, :, 0:NG], gmax, NG, sg4)
                link(tt(pe4, LG[:, :, NG:].rearrange("p t (g e) -> p t g e", g=NG),
                        ohg.unsqueeze(3).to_broadcast([P, 3, NG, 8]), ALU.mult))
                link(v.tensor_reduce(el, pe4.rearrange("p t g e -> p t e g"), AXX, ALU.add))
                link(v.tensor_reduce(v1, el, AXX, ALU.max))
                first_max(oh1, el, v1, 8, s8)
                link(stt(out=el, in0=oh1, scalar=-3e38, in1=el, op0=ALU.mult, op1=ALU.add))
                link(v.tensor_reduce(v2, el, AXX, ALU.max))
                tt(w2, v2, v1, ALU.subtract).then_inc(s("route_in"), 1)
                first_max(oh2, el, v2, 8, s8)
                v.wait_ge(s("route_exp"), 2 * y + 1)
                link(v.tensor_reduce(gsum, eg, AXX, ALU.add))
                v.wait_ge(s("route_exp"), 2 * y + 2)
                link(v.tensor_scalar(w1, w2, 1.0, None, ALU.add))
                link(tt(w1, w1, gsum, ALU.mult))
                link(v.reciprocal(w1, w1))
                link(tt(w2, w2, w1, ALU.mult))
                for o, oh in ((O1, oh1), (O2, oh2)):
                    for g in range(NG):
                        ins = tt(o[:, :, 8 * g:8 * g + 8], oh, ohg[:, :, g:g + 1].to_broadcast([P, 3, 8]), ALU.mult)
                link(ins)
                tt(AA, O1, O2, ALU.add).then_inc(s("A_set"), 1)
                link(tt(WT, O1, wide3(w1, NE), ALU.mult))
                link(tt(pe4.rearrange("p t g e -> p t (g e)"), O2, wide3(w2, NE), ALU.mult))
                link(tt(WT, WT, pe4.rearrange("p t g e -> p t (g e)"), ALU.add))
                v.tensor_copy(io, iota_i[:, :])
                v.tensor_copy(tokf, tok_i[:, :])
                for i in range(5):
                    ins = v.memset(lims[:, i:i + 1], float(SLOTS * i))
                link(ins)
                v.tensor_copy(VV[:, :, :, 0], wide3(tokf, NPAIR))
                v.memset(VV[:, :, :, 1], 1.0)
                v.tensor_copy(VV[:, :, :, 2:4], O2.rearrange("p t (i x) -> p t i x", x=2))
                link(v.tensor_copy(VV[:, :, :, 4:6], WT.rearrange("p t (i x) -> p t i x", x=2)))
                v.wait_ge(s("rk_done"), y + 1)
                link(v.tensor_reduce(cmx, ps[:, 7, 96:128], AXX, ALU.max))
                link(stt(out=RM, in0=ps[:, 7, 0:96].rearrange("p (t e) -> p t e", t=3), scalar=1.0, in1=AA,
                         op0=ALU.add, op1=ALU.mult))
                link(v.tensor_scalar(RM, RM, -1.0, None, ALU.add))
                link(v.tensor_scalar(cmp5, lims, cmx, None, ALU.is_lt))
                link(v.tensor_reduce(cmx, cmp5, AXX, ALU.add))
                v.tensor_copy(np_i[:, y:y + 1], cmx).then_inc(s("npass"), 1)
                v.wait_ge(s("npass"), y + 1)
                passes = v_passes[y] = v.value_load(np_i[0:1, y:y + 1], min_val=1, max_val=5)
                with v.Fori(0, passes) as q:
                    for n in range(3):
                        ins = tt(R[:, n], io.unsqueeze(1).to_broadcast([P, NE, SLOTS]),
                                 RM[:, n].unsqueeze(2).to_broadcast([P, NE, SLOTS]), ALU.is_equal)
                    ins.then_inc(s("R_set"), 1)
                    v.wait_ge(s("tb_done"), q + p0 + 1)
                    v.tensor_scalar(RM, RM, float(-SLOTS), None, ALU.add).then_inc(s("tbl"), 1)
                    v.tensor_copy(TB.rearrange("p i x -> p (i x)"), ps[:, 6, 0:6 * NPAIR]).then_inc(s("tbl"), 1)
                    v.wait_ge(s("tbl"), (q + p0) * 6 + 2)
                    for h in range(2):
                        r = slice(64 * h, 64 * h + 64)
                        v.tensor_copy(K2[r], TB[r, :, 2 + h])
                        v.tensor_copy(WS[r], TB[r, :, 4 + h])
                    stt(out=GI, in0=TB[:, :, 1], scalar=-FAR, in1=TB[:, :, 0], op0=ALU.mult, op1=ALU.add) \
                        .then_inc(s("tbl"), 1)
                    v.wait_ge(s("tbl"), (q + p0) * 6 + 3)
                    v.tensor_scalar(GI, GI, FAR, None, ALU.add).then_inc(s("tbl"), 1)
                    v.wait_ge(s("tbl"), (q + p0) * 6 + 4)
                    v.tensor_copy(GU, GI)
                    stt(out=SI, in0=K2, scalar=float(T), in1=GI, op0=ALU.mult, op1=ALU.add).then_inc(s("tbl"), 1)
                    v.wait_ge(s("tbl"), (q + p0) * 6 + 5)
                    v.tensor_copy(SU, SI).then_inc(s("tbl"), 1)
                    with v.Fori(0, NPAIR // 2) as n:
                        use = (q + p0) * (NPAIR // 2) + n
                        for b in range(2):
                            v.wait_ge(s("tbl"), (q + p0) * 6 + 6)
                            v.wait_ge(s(f"xg_ld{b}"), use * 16)
                            v.wait_ge(s(f"y_st{b}"), use * 16)
                            v.tensor_copy(gc[b], GU[:, bass.ds(2 * n + b, 1)])
                            v.tensor_copy(sc[b], SU[:, bass.ds(2 * n + b, 1)])
                            v.tensor_copy(wc[b], WS[:, bass.ds(2 * n + b, 1)]).then_inc(s(f"idx_set{b}"), 1)
                        for b in range(2):
                            i = 2 * use + b
                            v.wait_ge(s("xt_done"), i + 1)
                            v.tensor_copy(xgT[:, b, 4:8], ps[:, 1, :].rearrange("p (k t) -> p k t", k=4)) \
                                .then_inc(s("xtd"), 1)
                            v.wait_ge(s("sil"), i + 1)
                            tt(hid, sil, ps[:, 2, FF:2 * FF], ALU.mult).then_inc(s("hid"), 1)
                            v.wait_ge(s("rows_done"), i + 1)
                            v.wait_ge(s(f"idx_set{b}"), use + 1)
                            v.tensor_scalar(yst[:, b, 512:1024], ps[:, 5, :], wc[b], None, ALU.mult) \
                                .then_inc(s(f"yd{b}"), 1)
                for n, (t0, cnt) in enumerate(TILES):
                    if y == 1 and n == 2:
                        v.wait_ge(s(f"ld_y{n}"), 32 * (y + 1))
                        continue
                    v.wait_ge(s(f"ld_y{n}"), 32 * (y + 1))
                    tt(yrow[0:cnt, n, 0], yrow[0:cnt, n, 0], yrow[0:cnt, n, 1], ALU.add) \
                        .then_inc(s("y_sum"), 1)

            res_add(0)
            experts(0)
            for i in range(5):
                v.wait_ge(s("h_tr"), i + 6)
                if i < 4:
                    t0 = TILES[i // 2][0]
                    k0 = 4 * (i % 2)
                    dst, src = hT[:, k0:k0 + 4, t0:t0 + P], ps[:, i, :].rearrange("p (k t) -> p k t", k=4)
                else:
                    dst, src = hT[:, :, 0:META], ps[:, 4, 0:P].rearrange("p (k t) -> p k t", k=8)
                tt(dst, dst, src, ALU.add).then_inc(s("h_ready"), 1)
            if upto < 2:
                return
            v.wait_ge(s("nss"), 2)
            v.memset(xnO[:, :, 0:PAD], 0.0)
            norm(2, 1, rsO, xnO[:, :, PAD:TP])
            for x in (qO, kO, EA):
                v.memset(x[:, :, 0:PAD], 0.0)
            link(v.memset(LA[:, :, 0:PAD], 0.0))
            link(v.memset(QH, 0.0))
            link(v.memset(KH, 0.0))
            v.sem_inc(s("opads"), 1)
            v.wait_ge(s("gln"), 1)
            link(v.tensor_scalar(LA, LA, 0.0, None, ALU.min))
            link(tt(LA, LA, EA, ALU.subtract))
            link(v.tensor_scalar(LA, LA, 1.0 / 16, None, ALU.mult))
            flat = lambda x: x.rearrange("p j t -> p (j t)")
            v.tensor_tensor_scan(flat(CU), reset[:, :], flat(LA), 0.0, ALU.mult, ALU.add).then_inc(s("cu_set"), 1)
            v.wait_ge(s("cu_set"), 1)
            cc = CU.rearrange("p j (c t) -> p (j c) t", t=L)
            tt(EA.rearrange("p j (c t) -> p (j c) t", t=L), cc[:, :, L - 1:L].to_broadcast([P, 4 * NC, L]), cc,
               ALU.subtract).then_inc(s("kd_in"), 1)
            v.wait_ge(s("oproj_evac"), 9)
            v.wait_ge(s("ge"), 1)
            v.tensor_copy(elast[:, :, :], EB.rearrange("p j (c t) -> p j c t", t=L)[:, :, :, L - 1])
            link(tt(QE, qO, EB, ALU.mult))
            v.wait_ge(s("ge"), 2)
            tt(KDc, kO, EA, ALU.mult).then_inc(s("kd_set"), 1)
            v.wait_ge(s("kd_set"), 1)

            def halves(x, m):
                return flat(x).rearrange("p (b x r) -> p b x r", x=2, r=m)

            def level_in(i):
                m = L >> (i + 1)
                nb = SLAB // (2 * m)
                e, c = halves((EB, EA)[i % 2], m), halves(CU, m)
                ref = c[:, :, 0, m - 1:m].to_broadcast([P, nb, m])
                tt(e[:, :, 0], ref, c[:, :, 0], ALU.subtract)
                tt(e[:, :, 1], c[:, :, 1], ref, ALU.subtract).then_inc(s("lev_in"), 1)

            def pt_add(i):
                v.wait_ge(s("pt_done"), i + 1)
                mask = id64[:, :] if i == 0 else m_lev[:, 6 - i]
                for rows, sl, bk, n in ((slice(0, P), slice(0, 2), 2 * (i % 2), 8), (slice(0, 64), slice(2, 3), 2 * (i % 2) + 1, 4)):
                    dst = (PT if i == 0 else PTt)[rows, sl].rearrange("p s h t -> p (s h) t")
                    mk = mask[rows].unsqueeze(1).to_broadcast([rows.stop, n, L])
                    ins = tt(dst, ps[rows, bk, 0:n * L].rearrange("p (x t) -> p x t", t=L), mk, ALU.mult)
                ins.then_inc(s("pt_used"), 1)
                v.wait_ge(s("pt_used"), i + 1)
                if i:
                    tt(PT[:, 0:2], PT[:, 0:2], PTt[:, 0:2], ALU.add)
                    link(tt(PT[0:64, 2], PT[0:64, 2], PTt[0:64, 2], ALU.add))

            level_in(0)
            for i in range(6):
                m = L >> (i + 1)
                if i < 5:
                    level_in(i + 1)
                v.wait_ge(s("lev_e"), i + 1)
                if i >= 1:
                    v.wait_ge(s("pt_done"), i + 1)
                e = halves((EB, EA)[i % 2], m)
                tt(halves(KH, m)[:, :, 0], halves(kO, m)[:, :, 0], e[:, :, 0], ALU.mult)
                tt(halves(QH, m)[:, :, 1], halves(qO, m)[:, :, 1], e[:, :, 1], ALU.mult).then_inc(s("qk_set"), 1)
                v.wait_ge(s("qk_set"), i + 1)
                pt_add(i)
            pt_add(6)
            v.memset(SG, 0.0).then_inc(s("sg_set"), 1)
            for c in range(NC - 1):
                v.wait_ge(s("sg_done"), c + 1)
                v.wait_ge(s("og_done"), c + 1)
                v.wait_ge(s("sg_set"), 4 * c + 1)
                for h in range(4):
                    stt(out=SG[:, h], in0=SG[:, h], scalar=elast[:, h, c:c + 1],
                        in1=ps[:, 2 + h // 2, (h % 2) * 256:(h % 2) * 256 + 256], op0=ALU.mult, op1=ALU.add) \
                        .then_inc(s("sg_set"), 1)
            v.wait_ge(s("oproj_evac"), 29)
            for x in range(8):
                ins = v.tensor_scalar(rr[:, x], rr[:, x], col("gain", x), None, ALU.mult)
            link(ins)
            for h in range(4):
                v.wait_ge(s("og_rs"), h + 1)
                link(v.reciprocal(LA[:, h, 0:T], LA[:, h, 0:T]))
                for x in range(2):
                    link(tt(rr[:, 2 * h + x], rr[:, 2 * h + x], LA[:, h, 0:T], ALU.mult))
                    ins = tt(mixT[:, 2 * h + x], oG[:, 2 * h + x, PAD:TP], rr[:, 2 * h + x], ALU.mult)
            ins.then_inc(s("mix_ready"), 1)
            res_add(1)
            experts(1)
            v.wait_ge(s("ld_fn"), 16)
            v.wait_ge(s("y_sum"), 5)
            for n in range(2):
                v.wait_ge(s("hr_done"), n + 1)
                rows = yrow[:, n, 0].rearrange("p (d k) -> p k d", k=KD)
                for hf in range(2):
                    ins = tt(rows[:, 4 * hf:4 * hf + 4], rows[:, 4 * hf:4 * hf + 4],
                             ps[:, 2 * n + hf, :].rearrange("p (k d) -> p k d", k=4), ALU.add)
                ins.then_inc(s("fin_h"), 1)
            for n in range(2):
                v.wait_ge(s("fin_rs"), n + 1)
                link(v.reciprocal(fss[:, n:n + 1], fss[:, n:n + 1]))
                stt(out=yrow[:, n, 0], in0=yrow[:, n, 0], scalar=fss[:, n:n + 1], in1=fnb, op0=ALU.mult, op1=ALU.mult) \
                    .then_inc(s("out_set"), 1)


_INS = ['x', 'meta', 'e_norm', 'e_w_in', 'e_mu', 'e_decay0', 'e_decay_up', 'e_iclr0', 'e_iclr_up', 'e_gate_up', 'e_k_k',
        'e_k_a', 'e_r_k', 'e_ln_g', 'e_ln_b', 'e_conv_w', 'e_conv_b', 'e_lru_wa', 'e_lru_ba', 'e_lru_wx', 'e_lru_bx',
        'e_lru_lambda', 'e_w_out', 'o_norm', 'o_w_in', 'o_g_up', 'o_g_b', 'o_head_gain', 'o_w_out', 'm_norm',
        'm_w_group', 'm_b_group', 'm_w_router', 'm_b_router', 'm_w_gate', 'm_w_up', 'm_w_down', 'final_norm']


def kernel(**inputs):
    import numpy as _np
    import concourse.bacc as _bacc
    from concourse.bass_utils import run_bass_kernel_spmd as _run

    nc = _bacc.Bacc("TRN2", target_bir_lowering=False, num_devices=1)
    arrays, args = {}, {}
    for name in _INS:
        x = _np.ascontiguousarray(inputs[name])
        arrays[f"in_{name}_dram"] = x
        args[name] = nc.dram_tensor(f"in_{name}_dram", x.shape, mybir.dt.from_np(x.dtype), kind="ExternalInput").ap()
    out = nc.dram_tensor("out_0_dram", (1, SEQ, D), F32, kind="ExternalOutput").ap()
    xn_rows = nc.dram_tensor("xn_rows", (T, D), F32).ap()
    y_rows = nc.dram_tensor("y_rows", (2 * T, D), F32).ap()
    program(nc, args, out, xn_rows, y_rows)
    r = _run(nc, [arrays], core_ids=[0])
    return r.results[0]["out_0_dram"]
```

```python
from contextlib import ExitStack

import concourse.bass as bass
from concourse import mybir

ALU = mybir.AluOpType
ACT = mybir.ActivationFunctionType
AXX = mybir.AxisListType.X
F32 = mybir.dt.float32
BF16 = mybir.dt.bfloat16
I32 = mybir.dt.int32
U32 = mybir.dt.uint32

P = 128
D = 1024
KD = D // P
META = 16
SEQ = 256
T = META + SEQ
L = 64
NC = 5
TP = NC * L
PAD = TP - T
EPS = 1e-6
GN_EPS = 64e-5
E_IN = 2816
O_IN = 3088
NE = 32
NG = 4
FF = 256
NPAIR = NE // 2
NIT = NPAIR // 2
SLOTS = 64
SLAB = 4 * TP
FAR = 4096.0
TILES = [(META, P), (META + P, P), (0, META)]
PV = {}
_at = 0
for _name, _rows in (("mu", 14), ("decay0", 4), ("iclr0", 4), ("k_k", 4), ("k_a", 4), ("r_k", 4), ("ln_g", 4),
                     ("ln_b", 4), ("conv_w", 16), ("conv_b", 4), ("ba", 4), ("bx", 4), ("lam", 4), ("g_b", 4),
                     ("gain", 8)):
    PV[_name] = _at
    _at += _rows
NPV = _at
O_GROUPS = [(2048, 16), (0, 256), (256, 256), (512, 256), (768, 256)] + [(1024 + 256 * i, 256) for i in range(4)] \
    + [(2064 + 256 * i, 256) for i in range(4)]
O_UNITS = [1, 2, 2, 2, 2, 3, 3, 3, 3, 2, 2, 2, 2]
E_TILES = [14, 15, 16, 17, 18, 19, 20, 21, 12, 13, 4, 5, 6, 7, 0, 1, 2, 3, 8, 9, 10, 11]


def program(nc, a, out, y_dram):
    ctx = ExitStack()
    with ctx:
        def sb(name, shape, dt=F32):
            return ctx.enter_context(nc.sbuf_tensor(name, shape, dt))

        def sem(name):
            return ctx.enter_context(nc.semaphore(name))

        ps = ctx.enter_context(nc.psum_tensor("ps", [P, 8, 512], F32))
        RA = sb("RA", [P, 12288])
        W = sb("W", [P, 21 * SLAB])
        U = sb("U", [P, 8192])
        hT = sb("hT", [P, KD, T])
        ident = sb("ident", [P, P])
        ones = sb("ones", [P, P])
        onesbd = sb("onesbd", [P, P])
        id64 = sb("id64", [P, 64])
        before = sb("before", [P, P])
        m_ar = sb("m_ar", [P, 2, L])
        m_lev = sb("m_lev", [P, 6, L])
        reset = sb("reset", [P, SLAB], BF16)
        pv = sb("pv", [P, NPV])
        gains = sb("gains", [P, 4, KD])
        slam = sb("slam", [P, 8, 4])
        omka = sb("omka", [P, 4])
        epsb = sb("epsb", [P, 2])
        dlast = sb("dlast", [P, 4, NC])
        wr = sb("wr", [P, KD, NG + NE])
        BI = sb("BI", [P, NG + NE])
        np_i = sb("np_i", [P, 2], I32)
        iota_b = sb("iota_b", [P, SLOTS], BF16)
        rev = sb("rev", [P, 8])
        lims = sb("lims", [P, 5])
        tok_i = sb("tok_i", [P, 3], I32)
        tok_l = sb("tok_l", [P, 3], I32)
        tokp = sb("tokp", [P, 2, 3])

        def arr(first, *dims):
            n = 1
            for d in dims:
                n *= d
            v = W[:, first * SLAB:first * SLAB + n]
            names = " ".join("abcdef"[:len(dims)])
            return v.rearrange(f"p ({names}) -> p {names}", **{"abcdef"[i]: d for i, d in enumerate(dims)}) \
                if len(dims) > 1 else v

        block = ctx.enter_context(nc.Block())
        S = {}

        def s(name):
            if name not in S:
                S[name] = sem(name)
            return S[name]

        xtok = U[:, 0:3 * D].rearrange("p (t d) -> p t d", t=3)
        xnE = arr(19, KD, T)
        rT, kT, vT, aT, LW, CUM, EX, KK, KM = (arr(i, 4, TP) for i in (0, 1, 2, 3, 17, 18, 6, 7, 8))
        AR = arr(9, 4, NC, 2, L)
        Kt, Bt, BV, GT = (arr(i, 4, TP) for i in (11, 12, 13, 14))
        mixT = arr(15, 8, T)
        MA = arr(19, NC, 4, 2, L)
        MB = arr(17, NC, 4, 2, L)
        CT = arr(1, NC, 4, L)
        X, XT, YY = (arr(i, NC, 4, L) for i in (3, 4, 5))
        Vtk, Ktk, Btk = (arr(i, NC, 4, L) for i in (6, 7, 8))
        RH = W[:, 2 * SLAB:2 * SLAB + 256].rearrange("p (j v) -> p j v", j=4)
        nSA = W[:, 2 * SLAB + 256:2 * SLAB + 512].rearrange("p (j v) -> p j v", j=4)
        oT = arr(11, 4, TP)
        ST = W[:, 12 * SLAB:12 * SLAB + 256].rearrange("p (j v) -> p j v", j=4)
        STn = W[:, 12 * SLAB + 256:12 * SLAB + 512].rearrange("p (j v) -> p j v", j=4)
        raw = W[:, 4 * SLAB:4 * SLAB + 4 * 273].rearrange("p (s t) -> p s t", s=4)
        WA, GD, DT = (W[:, 5 * SLAB + i * T:5 * SLAB + (i + 1) * T] for i in range(3))
        rs = W[:, 6 * SLAB:6 * SLAB + T]
        xb, gb, xc, ga, gi, t1, t2, hh, aa = (arr(i, 4, T + 3 if i == 9 else T) for i in (9, 10, 11, 12, 13, 17, 18, 7, 8))
        lora = W[:, 14 * SLAB + 512:14 * SLAB + 1024]
        pvr = W[:, 14 * SLAB + 1024:14 * SLAB + 1152]
        gup = W[:, 14 * SLAB:14 * SLAB + 512]
        lruw = sb("lruw", [P, 2, 4, L])
        wring = RA[:, :].rearrange("p (s k c) -> p s k c", s=6, k=KD)
        wout = U[:, :].rearrange("p (k d) -> p k d", k=KD)
        sq = xnE

        xnO = arr(19, KD, TP)
        qO, kO = arr(0, 4, TP), arr(1, 4, TP)
        rr = arr(2, 8, T)
        Vo = arr(4, 3, D)
        rsO = W[:, 6 * SLAB + 600:6 * SLAB + 600 + T]
        LA, CU, QE, KDc, EA, QH, KH = (arr(i, 4, TP) for i in (7, 8, 9, 10, 11, 12, 13))
        EB = arr(18, 4, TP)
        PT = arr(14, 3, 4, L)
        PTt = W[:, 17 * SLAB:17 * SLAB + 768].rearrange("p (s h t) -> p s h t", s=3, h=4)
        gdT = W[0:16, 14 * SLAB + 800:14 * SLAB + 800 + T]
        kdt = arr(15, 3, 4, P)
        SG = [arr(17, 4, FF), arr(18, 4, FF)]
        oG = arr(12, 8, TP)
        sqG = arr(10, 8, T)
        elast = sb("elast", [P, 4, NC])
        gupO = sb("gupO", [16, 4 * P])
        PLACE = {1: (0, 0), 2: (0, 1), 3: (1, 0), 4: (1, 1), 0: (2, 0)}

        slot_w = [RA[:, 0:12288].rearrange("p (e w) -> p e w", e=2), W[:, 0:12288].rearrange("p (e w) -> p e w", e=2)]
        xpart = U[:, 0:3072].bitcast(BF16).rearrange("p (t x d) -> p t x d", t=2, x=3)
        xmeta = U[0:96, 3072:3584].bitcast(BF16)
        xgT = U[:, 3584:5632].rearrange("p (k t) -> p k t", k=KD)
        sil, hid = U[:, 5632:5888], U[:, 5888:6144]
        hidT = U[:, 6144:6400].rearrange("p (k t) -> p k t", k=2)
        Rb = U[:, 6400:6656].bitcast(BF16).rearrange("p (t c) -> p t c", t=2)
        Rm = U[0:96, 6656:6784].bitcast(BF16)
        tbs = U[:, 6784:6806].rearrange("p (b x) -> p b x", b=2)
        sel = U[:, 6806:6814].rearrange("p (b x) -> p b x", b=2)
        ix = U[:, 6816:6818]
        inext, icur = (U[:, i:i + 2].bitcast(U32) for i in (6820, 6822))
        wnext, wcur = U[:, 6824:6826], U[:, 6826:6828]
        yst = W[:, 12288:14336].rearrange("p (s d) -> p s d", s=2)
        rest = W[:, 14336:17408].rearrange("p (u d) -> p u d", u=6)
        AT = [slice(0, P), slice(0, P), slice(32, 32 + META)]
        yrow = W[:, 12288:18432].rearrange("p (t x d) -> p t x d", t=3, x=2)
        at = [18432]

        def rt(*dims, dt=F32):
            n = 1
            for d in dims:
                n *= d
            w = n if dt != BF16 else (n + 1) // 2
            v = W[:, at[0]:at[0] + w]
            at[0] += w
            if dt != F32:
                v = v.bitcast(dt)[:, 0:n]
            names = " ".join("abcd"[:len(dims)])
            return v.rearrange(f"p ({names}) -> p {names}", **{"abcd"[i]: d for i, d in enumerate(dims)}) \
                if len(dims) > 1 else v

        rsM = rt(T)
        LG = rt(3, NG + NE)
        gmax, gsum, v1, v2, w1, w2 = (rt(3) for _ in range(6))
        eg, ohg, sg4 = rt(3, NG), rt(3, NG), rt(3, NG)
        pe4 = rt(3, NG, 8)
        el, oh1, oh2, s8 = (rt(3, 8) for _ in range(4))
        O1, O2, AA, WT, RM = (rt(3, NE) for _ in range(5))
        RMx = rt(NE)
        cmp5, cmx = rt(5), rt(1)
        VV = rt(3, NPAIR, 12, dt=BF16)
        fnb = arr(0, D)
        fss = rt(2)
        assert at[0] <= 19 * SLAB

        @block.sync
        def _(sp):
            sp_passes = {-1: 0}
            for n, (t0, cnt) in enumerate(TILES):
                src = a["x"][0, t0 - META:t0 - META + cnt, :] if t0 else a["meta"]
                sp.dma_start(xtok[0:cnt, n, :], src).then_inc(s("ld_x"), 16)
            w_in = a["e_w_in"][0].rearrange("(p k) c -> p k c", k=KD)
            for g in range(11):
                if g >= 6:
                    sp.wait_ge(s("proj_done"), 2 * (g - 5))
                c0 = E_TILES[2 * g] * P
                sp.dma_start(wring[:, g % 6], w_in[:, :, c0:c0 + 2 * P]).then_inc(s(f"ld_w{g % 6}"), 16)
            sp.wait_ge(s("h_ready"), 5)
            sp.dma_start(wout, a["e_w_out"][0].rearrange("(k p) d -> p k d", p=P)).then_inc(s("ld_wout"), 16)

            def experts(y):
                p0 = sp_passes[y - 1]
                gate, up = (a[key][y].rearrange("e (p k) f -> p e (k f)", k=KD) for key in ("m_w_gate", "m_w_up"))
                down = a["m_w_down"][y].rearrange("e (p k) d -> p e (k d)", k=2)

                def pair(slot, i, it):
                    sp.wait_ge(s("gu_done"), 2 * it + slot + 1)
                    sp.dma_start(slot_w[slot][:, :, 0:2048], gate[:, bass.ds(i, 2), :]).then_inc(s(f"ld_gu{slot}"), 16)
                    sp.dma_start(slot_w[slot][:, :, 2048:4096], up[:, bass.ds(i, 2), :]).then_inc(s(f"ld_gu{slot}"), 16)
                    sp.wait_ge(s("rows_done"), 2 * it + slot + 1)
                    sp.dma_start(slot_w[slot][:, :, 4096:6144], down[:, bass.ds(i, 2), :]).then_inc(s(f"ld_d{slot}"), 16)

                first = p0 * NIT
                pair(0, 0, first)
                sp.wait_ge(s("res_add"), KD * (y + 1))
                pair(1, 2, first)
                with sp.Fori(1, NIT) as n:
                    for slot in range(2):
                        pair(slot, 4 * n + 2 * slot, n + first)
                sp.wait_ge(s("npass"), y + 1)
                passes = sp_passes[y] = sp.value_load(np_i[0:1, y:y + 1], min_val=1, max_val=5)
                with sp.If(passes > 1):
                    with sp.Fori(1, passes) as q:
                        with sp.Fori(0, NIT) as n:
                            for slot in range(2):
                                pair(slot, 4 * n + 2 * slot, (q + p0) * NIT + n)

            sp.wait_ge(s("proj_done"), 22)
            experts(0)
            sp.wait_ge(s("pe_end"), 1)
            sp.wait_ge(s("ld_y2"), 32)
            w_o = a["o_w_in"][0].rearrange("(p k) c -> p k c", k=KD)
            for g, (c0, w) in enumerate(O_GROUPS):
                if g >= 6:
                    sp.wait_ge(s("oproj"), sum(O_UNITS[:g - 5]))
                sp.dma_start(wring[:, g % 6, :, 0:w], w_o[:, :, c0:c0 + w]).then_inc(s(f"ld_w{g % 6}"), 16)
            sp.dma_start(wout, a["o_w_out"][0].rearrange("(k p) d -> p k d", p=P)).then_inc(s("ld_wout"), 16)
            sp.wait_ge(s("oproj"), sum(O_UNITS))
            experts(1)
            sp.wait_ge(s("pe_end"), 2)
            sp.dma_start(fnb, a["final_norm"].rearrange("(o d) -> o d", o=1).broadcast_to([P, D])).then_inc(s("ld_fn"), 16)
            for n in range(2):
                sp.wait_ge(s("out_set"), n + 1)
                sp.dma_start(out[0, n * P:(n + 1) * P, :], yrow[:, n, 0, :]).then_inc(s("st_out"), 16)
            sp.wait_ge(s("st_out"), 32)

        @block.scalar
        def _(act):
            act_passes = {-1: 0}
            n_link = [0]

            def link(ins):
                n_link[0] += 1
                ins.then_inc(s("act_chain"), 1)
                act.wait_ge(s("act_chain"), n_link[0])

            for name, key in (("mu", "e_mu"), ("decay0", "e_decay0"), ("iclr0", "e_iclr0"), ("k_k", "e_k_k"),
                              ("k_a", "e_k_a"), ("r_k", "e_r_k"), ("ln_g", "e_ln_g"), ("ln_b", "e_ln_b"),
                              ("conv_b", "e_conv_b"), ("ba", "e_lru_ba"), ("bx", "e_lru_bx"), ("lam", "e_lru_lambda"),
                              ("g_b", "o_g_b"), ("gain", "o_head_gain")):
                rows = a[key].shape[1] // P
                act.dma_start(pvr[PV[name]:PV[name] + rows, :],
                              a[key].rearrange("o (r c) -> (o r) c", c=P)).then_inc(s("ld_pv"), 16)
            act.dma_start(pvr[PV["conv_w"]:PV["conv_w"] + 16, :],
                          a["e_conv_w"].rearrange("o i (r c) -> (o i r) c", c=P)).then_inc(s("ld_pv"), 16)
            for n, v in enumerate((a["e_norm"][0], a["o_norm"][0], a["m_norm"][0], a["m_norm"][1])):
                act.dma_start(gains[:, n, :], v.rearrange("(p k) -> p k", k=KD)).then_inc(s("ld_gain"), 16)
            act.dma_start(lora[0:64, :], a["e_decay_up"][0]).then_inc(s("ld_lora"), 16)
            act.dma_start(lora[64:128, :], a["e_iclr_up"][0]).then_inc(s("ld_lora"), 16)
            act.dma_start(gup, a["e_gate_up"][0]).then_inc(s("ld_lora"), 16)
            for n, key in enumerate(("e_lru_wa", "e_lru_wx")):
                for h in range(2):
                    act.dma_start(lruw[64 * h:64 * h + 64, n],
                                  a[key][0].rearrange("(j h) i o -> h i j o", h=2)[h]).then_inc(s("ld_lruw"), 16)

            def load_router(y):
                act.dma_start(wr[:, :, 0:NG], a["m_w_group"][y].rearrange("(p k) c -> p k c", k=KD)).then_inc(s("ld_wr"), 16)
                act.dma_start(wr[:, :, NG:], a["m_w_router"][y].rearrange("(p k) c -> p k c", k=KD)).then_inc(s("ld_wr"), 16)
                act.dma_start(BI[:, 0:NG], a["m_b_group"][y:y + 1, :].broadcast_to([P, NG])).then_inc(s("ld_bi"), 16)
                act.dma_start(BI[:, NG:], a["m_b_router"][y:y + 1, :].broadcast_to([P, NE])).then_inc(s("ld_bi"), 16)

            load_router(0)
            act.wait_ge(s("h_ready"), 5)
            act.wait_ge(s("eps_set"), 1)
            for k in range(KD):
                nc.scalar.activation(sq[:, k], hT[:, k], ACT.Square).then_inc(s("sq0"), 1)
            act.wait_ge(s("aux_done"), 1)
            nc.scalar.activation(rs, ps[:, 4, 0:T], ACT.Sqrt, bias=epsb[:, 0:1], scale=1.0 / D).then_inc(s("aux_evac"), 1)
            act.wait_ge(s("lam_abs"), 1)
            nc.scalar.activation(slam[:, 1], slam[:, 0], ACT.Exp, scale=-1.0).then_inc(s("lam_exp"), 1)

            def evac(n):
                m = E_TILES[n]
                act.wait_ge(s("proj_done"), n + 1)
                src = ps[:, n % 4, 0:T]
                if 14 <= m < 18:
                    dst = xb[:, m - 14, 3:T + 3]
                elif m >= 18:
                    dst = gb[:, m - 18]
                else:
                    i = n - 8
                    if i == 0:
                        act.wait_ge(s("pads_zero"), 1)
                    if i >= 4:
                        act.wait_ge(s("shifted"), i - 3)
                    dst = raw[:, i % 4, 1:T + 1]
                nc.scalar.activation(dst, src, ACT.Copy).then_inc(s("proj_evac"), 1)

            def aux(u, *ins_of):
                act.wait_ge(s("aux_done"), u + 1)
                nc.scalar.activation(*ins_of[:3], **ins_of[3]).then_inc(s("aux_evac"), 1)

            for n in range(10):
                evac(n)
            for g in range(2):
                for j in range(4):
                    u = 1 + 4 * g + j
                    b = PV["ba" if g == 0 else "bx"] + j
                    aux(u, (ga, gi)[g][:, j], ps[:, 4 + u % 4, 0:T], ACT.Sigmoid, dict(bias=pv[:, b:b + 1]))
            act.wait_ge(s("shifted"), 2)
            nc.scalar.activation(WA[0:64, :], WA[0:64, :], ACT.Tanh).then_inc(s("lora_in"), 1)
            nc.scalar.activation(GD[:, :], GD[:, :], ACT.Sigmoid).then_inc(s("lora_in"), 1)
            evac(10)
            act.wait_ge(s("slam_set"), 1)
            act.wait_ge(s("aux_evac"), 9)
            for j in range(4):
                nc.scalar.activation(aa[:, j], ga[:, j], ACT.Exp, scale=slam[:, 5, j:j + 1]).then_inc(s("lru_a"), 1)
            for j in range(4):
                nc.scalar.activation(t1[:, j], ga[:, j], ACT.Tanh, scale=slam[:, 5, j:j + 1]).then_inc(s("lru_a"), 1)
            act.wait_ge(s("lru_in"), 1)
            nc.scalar.activation(t2, t2, ACT.Tanh, scale=0.7978845608028654).then_inc(s("lru_a"), 1)
            evac(11)
            evac(12)
            act.wait_ge(s("lru_in"), 2)
            nc.scalar.activation(t1, t1, ACT.Sqrt, scale=-1.0).then_inc(s("lru_a"), 1)
            for n in range(13, 18):
                evac(n)
            act.wait_ge(s("pads_zero"), 1)
            for j in range(4):
                u = 9 + j
                aux(u, EX[:, j, PAD:TP], ps[:, 4 + u % 4, 0:T], ACT.Sigmoid,
                    dict(bias=pv[:, PV["decay0"] + j:PV["decay0"] + j + 1]))
            for j in range(4):
                u = 13 + j
                aux(u, aT[:, j, PAD:TP], ps[:, 4 + u % 4, 0:T], ACT.Sigmoid,
                    dict(bias=pv[:, PV["iclr0"] + j:PV["iclr0"] + j + 1]))
            for j in range(4):
                u = 17 + j
                act.wait_ge(s("aux_done"), 21)
                aux(u, GT[:, j, PAD:TP], ps[:, 4 + u % 4, 0:T], ACT.Copy, {})
            evac(18)
            evac(19)
            for j in range(4):
                u = 21 + j
                aux(u, Kt[:, j], ps[:, 4 + u % 4, 0:TP], ACT.Sqrt, {})
            act.wait_ge(s("cum_set"), 1)
            nc.scalar.activation(EX, LW, ACT.Exp).then_inc(s("exps"), 1)
            evac(20)
            act.wait_ge(s("ex_used"), 1)
            nc.scalar.activation(EX, CUM, ACT.Exp).then_inc(s("exps"), 1)
            evac(21)
            act.wait_ge(s("ex_used"), 2)
            nc.scalar.activation(EX, CUM, ACT.Exp, scale=-1.0).then_inc(s("exps"), 1)
            for j in range(4):
                u = 25 + j
                aux(u, BV[:, j], ps[:, 4 + u % 4, 0:TP], ACT.Copy, {})
            for c in range(NC):
                act.wait_ge(s("pm_done"), c + 1)
                nc.scalar.activation(Vtk[:, c], ps[:, 2, 256:512].rearrange("p (j v) -> p j v", j=4), ACT.Copy)
                nc.scalar.activation(Ktk[:, c], ps[:, 3, 0:256].rearrange("p (j v) -> p j v", j=4), ACT.Copy)
                nc.scalar.activation(Btk[:, c], ps[:, 3, 256:512].rearrange("p (j v) -> p j v", j=4),
                                     ACT.Copy).then_inc(s("tok_evac"), 1)
            for n in range(5 * NC):
                act.wait_ge(s("y_done"), n + 1)
                nc.scalar.activation(YY[:, n % NC], ps[:, 4 + n % 2, 0:256].rearrange("p (j v) -> p j v", j=4),
                                     ACT.Copy).then_inc(s("y_evac"), 1)
            for c in range(NC):
                act.wait_ge(s("rh_done"), c + 1)
                nc.scalar.activation(RH, ps[:, 0, 0:256].rearrange("p (j v) -> p j v", j=4), ACT.Copy) \
                    .then_inc(s("rh_evac"), 1)
                act.wait_ge(s("sa_done"), c + 1)
                nc.scalar.activation(nSA, ps[:, 1, 0:256].rearrange("p (j v) -> p j v", j=4), ACT.Copy, scale=-1.0) \
                    .then_inc(s("sa_evac"), 1)
                act.wait_ge(s("o_done"), c + 1)
                nc.scalar.activation(oT[:, :, c * L:(c + 1) * L], ps[:, 2, 0:256].rearrange("p (j v) -> p j v", j=4),
                                     ACT.Copy).then_inc(s("o_evac"), 1)
            for j in range(4):
                u = 29 + j
                aux(u, LW[:, j, 0:T], ps[:, 4 + u % 4, 0:T], ACT.Copy, dict(scale=1.0 / L))
            for j in range(4):
                u = 33 + j
                aux(u, CUM[:, j, 0:T], ps[:, 4 + u % 4, 0:T], ACT.Sqrt, dict(bias=epsb[:, 1:2], scale=1.0 / L))

            def norm(i, dst, scratch, after):
                for k in range(KD):
                    act.wait_ge(s(after[0]), after[1] + (k if after[0] == "res_add" else 0))
                    nc.scalar.activation(sq[:, k], hT[:, k], ACT.Square).then_inc(s("nsq"), 1)
                act.wait_ge(s("nss"), i)
                nc.scalar.activation(scratch, ps[:, 7, 0:T], ACT.Sqrt, bias=epsb[:, 0:1], scale=1.0 / D) \
                    .then_inc(s("nrs"), 1)

            def experts(y):
                p0 = act_passes[y - 1]
                norm(2 * y + 1, xnE, rsM, ("res_add", KD * y + 1))
                for n, (t0, cnt) in enumerate(TILES):
                    act.wait_ge(s("row_tr"), 3 * y + n + 1)
                    if n == 2:
                        act.wait_ge(s("route_in"), 2 * y + 1)
                        nc.scalar.activation(eg, eg, ACT.Exp).then_inc(s("route_exp"), 1)
                        act.wait_ge(s("route_in"), 2 * y + 2)
                        nc.scalar.activation(w2, w2, ACT.Exp).then_inc(s("route_exp"), 1)
                        act.wait_ge(s("xm_set"), y + 1)
                    for hf in range(2):
                        src, c = ps[0:cnt, 2 * n + hf, :], slice(hf * 512, hf * 512 + 512)
                        dst = xpart[:, n, 0, c] if n < 2 else xmeta[0:META, c]
                        if n == 2:
                            nc.scalar.activation(xmeta[32:32 + META, c], src, ACT.Copy)
                        nc.scalar.activation(rest[AT[n], 2 * n + hf], src, ACT.Copy)
                        nc.scalar.activation(dst, src, ACT.Copy).then_inc(s("part1"), 1)
                for n in range(3):
                    for hf in range(2):
                        act.wait_ge(s("rest1"), 6 * y + 2 * n + hf + 1)
                        c = slice(hf * 512, hf * 512 + 512)
                        dst = xpart[:, n, 1, c] if n < 2 else xmeta[32:32 + META, c]
                        nc.scalar.activation(dst, rest[AT[n], 2 * n + hf], ACT.Copy).then_inc(s("part2"), 1)
                act.wait_ge(s("npass"), y + 1)
                passes = act_passes[y] = act.value_load(np_i[0:1, y:y + 1], min_val=1, max_val=5)

                def gathered(it):
                    act.wait_ge(s("g_done"), it + 1)
                    for b in range(2):
                        ins = nc.scalar.activation(xgT[:, 2 * b:2 * b + 2], ps[:, b, :].rearrange("p (k t) -> p k t", k=2),
                                                   ACT.Copy)
                    ins.then_inc(s("xga"), 1)

                def tables(it):
                    act.wait_ge(s("tb_done"), it + 1)
                    nc.scalar.activation(tbs, ps[:, 5, 256:278].rearrange("p (b x) -> p b x", b=2), ACT.Copy) \
                        .then_inc(s("tb_evac"), 1)

                def step(it, more):
                    for b in range(2):
                        i = 2 * it + b
                        act.wait_ge(s("gu_done"), i + 3)
                        nc.scalar.activation(sil, ps[:, 4, 0:FF], ACT.Silu).then_inc(s("sil"), 1)
                        if b == 1 and more:
                            gathered(it + 1)
                        if b == 0 and more:
                            tables(it + 1)
                        act.wait_ge(s("ht_done"), i + 1)
                        nc.scalar.activation(hidT, ps[:, 5, 0:FF].rearrange("p (k t) -> p k t", k=2),
                                             ACT.Copy).then_inc(s("hte"), 1)
                        act.wait_ge(s("rows_done"), i + 3)
                        act.wait_ge(s("idx_set"), i + 1)
                        act.wait_ge(s(f"y_free{b}"), it + 1)
                        nc.scalar.activation(yst[:, b, 0:512], ps[:, 6, :], ACT.Copy, scale=wcur[:, b:b + 1]) \
                            .then_inc(s("ya"), 1)

                with act.Fori(0, passes) as q:
                    tables((q + p0) * NIT)
                    gathered((q + p0) * NIT)
                    with act.Fori(0, NIT - 1) as n:
                        step((q + p0) * NIT + n, True)
                    step((q + p0) * NIT + NIT - 1, False)
                act.wait_ge(s("scat"), y + 1)
                for n, (t0, cnt) in enumerate(TILES):
                    for x in range(2):
                        act.dma_start(yrow[0:cnt, n, x, :], y_dram[x * T + t0:x * T + t0 + cnt, :]) \
                            .then_inc(s(f"ld_y{n}"), 16)

            act.sem_inc(s("ya"), 1)
            experts(0)
            load_router(1)
            act.dma_start(gupO[:, :], a["o_g_up"][0]).then_inc(s("ld_gupO"), 16)
            norm(2, xnO, rsO, ("h_ready", 10))
            for n in range(29):
                act.wait_ge(s("oproj"), n + 1)
                b = ps[:, n % 4]
                if n == 0:
                    args = (gdT, b[0:16, 0:T], ACT.Copy)
                elif n < 5:
                    args = (qO[:, n - 1, PAD:TP], b[:, 0:T], ACT.Copy)
                elif n < 9:
                    args = (kO[:, n - 5, PAD:TP], b[:, 0:T], ACT.Copy)
                elif n < 21:
                    g, t = (n - 9) // 3, (n - 9) % 3
                    rows = 64 if t == 2 else P
                    args = (Vo[0:rows, t, g * 256:(g + 1) * 256], b[0:rows, 0:256], ACT.Copy)
                else:
                    args = (rr[:, n - 21], b[:, 0:T], ACT.Silu)
                nc.scalar.activation(*args, **(dict(scale=float(P) ** -0.5) if 1 <= n < 5 else {})) \
                    .then_inc(s("oproj_evac"), 1)
                if n == 8:
                    act.wait_ge(s("opads"), 1)
                    for j in range(4):
                        act.wait_ge(s("gx"), j + 1)
                        b0 = PV["g_b"] + j
                        nc.scalar.activation(LA[:, j, PAD:TP], ps[:, 4 + j, 0:T], ACT.Identity, bias=pv[:, b0:b0 + 1]) \
                            .then_inc(s("gx_evac"), 1)
                    act.wait_ge(s("gx_evac"), 4)
                    link(nc.scalar.activation(EA[:, :, PAD:TP], LA[:, :, PAD:TP], ACT.Abs))
                    link(nc.scalar.activation(EA[:, :, PAD:TP], EA[:, :, PAD:TP], ACT.Exp, scale=-1.0))
                    nc.scalar.activation(EA[:, :, PAD:TP], EA[:, :, PAD:TP], ACT.Ln, bias=1.0).then_inc(s("gln"), 1)
                if n == 10:
                    act.wait_ge(s("cu_set"), 1)
                    nc.scalar.activation(EB, CU, ACT.Exp).then_inc(s("ge"), 1)
                    act.wait_ge(s("kd_in"), 1)
                    nc.scalar.activation(EA, EA, ACT.Exp).then_inc(s("ge"), 1)
                if n == 13:
                    act.wait_ge(s("kdt_done"), 1)
                    for sl in range(3):
                        rows = 64 if sl == 2 else P
                        ins = nc.scalar.activation(kdt[0:rows, sl], ps[0:rows, 4 + sl, :].rearrange("p (h k) -> p h k", h=4),
                                                   ACT.Copy)
                    ins.then_inc(s("kdt_set"), 1)
                if n >= 12 and n % 2 == 0 and n < 24:
                    i = (n - 12) // 2
                    act.wait_ge(s("lev_in"), i + 1)
                    e = (EB, EA)[i % 2]
                    nc.scalar.activation(e, e, ACT.Exp).then_inc(s("lev_e"), 1)
            for i in range(NC):
                act.wait_ge(s("og_done"), i + 1)
                nc.scalar.activation(oG[:, :, i * L:(i + 1) * L], ps[:, i % 2, :].rearrange("p (x t) -> p x t", x=8),
                                     ACT.Copy).then_inc(s("og_evac"), 1)
            act.wait_ge(s("og_evac"), NC)
            for x in range(8):
                nc.scalar.activation(sqG[:, x], oG[:, x, PAD:TP], ACT.Square).then_inc(s("og_sq"), 1)
            for h in range(4):
                act.wait_ge(s("og_ss"), h + 1)
                nc.scalar.activation(LA[:, h, 0:T], ps[:, 4 + h, 0:T], ACT.Sqrt, bias=epsb[:, 0:1], scale=1.0 / 256) \
                    .then_inc(s("og_rs"), 1)
            experts(1)
            for n in range(2):
                act.wait_ge(s("fin_h"), n + 1)
                link(nc.scalar.activation(yrow[:, n, 1, :], yrow[:, n, 0, :], ACT.Square, accum_out=fss[:, n:n + 1]))
                nc.scalar.activation(fss[:, n:n + 1], fss[:, n:n + 1], ACT.Sqrt, bias=epsb[:, 0:1], scale=1.0 / D) \
                    .then_inc(s("fin_rs"), 1)

        @block.gpsimd
        def _(pool):
            pool_passes = {-1: 0}
            n_link = [0]

            def link(ins):
                n_link[0] += 1
                ins.then_inc(s("pool_chain"), 1)
                pool.wait_ge(s("pool_chain"), n_link[0])

            def keep(dst, src, pattern, base, mult=1, op=ALU.is_ge):
                link(pool.affine_select(out=dst, in_=src, pattern=pattern, compare_op=op, fill=0.0, base=base,
                                        channel_multiplier=mult))

            link(pool.memset(ones[:, :], 1.0))
            keep(ident[:, :], ones[:, :], [[-1, P]], 0, op=ALU.is_equal)
            keep(before[:, :], ones[:, :], [[1, P]], -1, mult=-1)
            pool.sem_inc(s("consts"), 1)
            link(pool.memset(onesbd[:, :], 0.0))
            for h in range(2):
                r = slice(64 * h, 64 * h + 64)
                link(pool.memset(onesbd[r, r], 1.0))
                keep(id64[r, :], ones[r, 0:64], [[-1, 64]], 0, op=ALU.is_equal)
                keep(m_ar[r, 0, :], ones[r, 0:64], [[1, L]], -1, mult=-1)
                keep(m_ar[r, 1, :], ones[r, 0:64], [[1, L]], 0, mult=-1)
            link(pool.memset(m_lev[:, :, :], 0.0))
            for h in range(2):
                r = slice(64 * h, 64 * h + 64)
                for lev in range(6):
                    m = 1 << lev
                    nb = L // (2 * m)
                    dst = m_lev[r, lev, :].rearrange("p (b x r) -> p b x r", x=2, r=m)[:, :, 1, :]
                    one = ones[r, 0:nb * m].rearrange("p (b r) -> p b r", r=m)
                    keep(dst, one, [[-2 * m, nb], [0, m]], 0)
                    keep(dst, dst, [[2 * m, nb], [0, m]], m - 1, mult=-1)
            for b in range(2):
                pool.sem_inc(s(f"y_free{b}"), 1)
            pool.iota(iota_b[:, :], [[1, SLOTS]], base=0, channel_multiplier=0, allow_small_or_imprecise_dtypes=True)
            for i in range(8):
                pool.memset(rev[:, i:i + 1], float(8 - i))
            for i in range(5):
                pool.memset(lims[:, i:i + 1], float(SLOTS * i))
            for n, (t0, _) in enumerate(TILES):
                link(pool.iota(tok_i[:, n:n + 1], [[1, 1]], base=t0, channel_multiplier=1))
            pool.sem_inc(s("consts"), 1)

            def experts(y):
                p0 = pool_passes[y - 1]
                for n, (_, cnt) in enumerate(TILES):
                    for hf in range(2):
                        pool.wait_ge(s("part1"), 6 * y + 2 * n + hf + 1)
                        if n == 2:
                            pool.wait_ge(s("rest1"), 6 * y + 2 * n + hf)
                        c = slice(hf * 512, hf * 512 + 512)
                        one = xpart[:, n, 0, c] if n < 2 else xmeta[32:32 + META, c]
                        pool.tensor_tensor(rest[AT[n], 2 * n + hf], rest[AT[n], 2 * n + hf], one, ALU.subtract) \
                            .then_inc(s("rest1"), 1)
                pool.wait_ge(s("rest1"), 6 * y + 6)
                for n, (_, cnt) in enumerate(TILES):
                    for hf in range(2):
                        pool.wait_ge(s("part2"), 6 * y + 2 * n + hf + 1)
                        if n == 2:
                            pool.wait_ge(s("part3"), 6 * y + 2 * n + hf)
                        c = slice(hf * 512, hf * 512 + 512)
                        two = xpart[:, n, 1, c] if n < 2 else xmeta[32:32 + META, c]
                        three = xpart[:, n, 2, c] if n < 2 else xmeta[64:64 + META, c]
                        pool.tensor_tensor(three, rest[AT[n], 2 * n + hf], two, ALU.subtract).then_inc(s("part3"), 1)
                pool.wait_ge(s("npass"), y + 1)
                passes = pool_passes[y] = pool.value_load(np_i[0:1, y:y + 1], min_val=1, max_val=5)
                last_out = pool.to_reg(2 * T - 1)
                with pool.Fori(0, passes) as q:
                    with pool.Fori(0, NIT) as n:
                        it = (q + p0) * NIT + n
                        for b in range(2):
                            pool.wait_ge(s("ya"), 2 * it + b + 2)
                            pool.wait_ge(s("yd"), 2 * it + b + 2)
                            pool.sem_inc(s("pool_go"), 1)
                            pool.indirect_dma_start(out=y_dram, out_offset=bass.IndirectOffsetOnAxis(ap=icur[:, b:b + 1], axis=0),
                                                    in_=yst[:, b, :], in_offset=None,
                                                    bounds_check=last_out, oob_is_err=False).then_inc(s(f"y_st{b}"), 16)
                        for b in range(2):
                            pool.wait_ge(s(f"y_st{b}"), it * 16 + 16)
                            pool.sem_inc(s(f"y_free{b}"), 1)
                pool.sem_inc(s("scat"), 1)

            for y in range(2):
                experts(y)

        @block.tensor
        def _(pe):
            pe_passes = {-1: 0}
            pe.sem_inc(s("gu_done"), 2)
            pe.sem_inc(s("rows_done"), 2)
            pe.wait_ge(s("ld_x"), 48)
            pe.wait_ge(s("consts"), 1)
            for n, (t0, cnt) in enumerate(TILES):
                for k in range(KD):
                    b = 2 * n + k // 4 if n < 2 else 4
                    o = ps[:, b, (k % 4) * P:(k % 4) * P + cnt] if n < 2 else ps[:, b, k * META:(k + 1) * META]
                    ins = pe.transpose(o, xtok[0:cnt, n, k::KD], ident[0:cnt, 0:cnt])
                    if k % 4 == 3 and (n < 2 or k == 7):
                        ins.then_inc(s("h_tr"), 1)
            pe.wait_ge(s("ld_pv"), 240)
            pe.transpose(ps[:, 5, 0:NPV], pvr[0:NPV, :], ident[0:NPV, 0:NPV]).then_inc(s("pv_tr"), 1)
            pe.wait_ge(s("h_ready"), 5)
            for k in range(KD):
                pe.wait_ge(s("sq0"), k + 1)
                ins = pe.matmul(ps[:, 4, 0:T], ones[:, :], sq[:, k], start=(k == 0), stop=(k == KD - 1))
            ins.then_inc(s("aux_done"), 1)
            pe.wait_ge(s("pv_set"), 1)

            def proj(n):
                if n >= 4:
                    pe.wait_ge(s("proj_evac"), n - 3)
                if n % 2 == 0:
                    g = n // 2
                    pe.wait_ge(s(f"ld_w{g % 6}"), 16 * (g // 6 + 1))
                for k in range(KD):
                    if n == 0:
                        pe.wait_ge(s("xn0"), k + 1)
                    ins = pe.matmul(ps[:, n % 4, 0:T], wring[:, (n // 2) % 6, k, (n % 2) * P:(n % 2) * P + P],
                                    xnE[:, k], start=(k == 0), stop=(k == KD - 1))
                ins.then_inc(s("proj_done"), 1)

            def aux(u, *pairs, n=T):
                if u >= 5:
                    pe.wait_ge(s("aux_evac"), u - 3)
                for out_rows, lhs, rhs in pairs:
                    ins = pe.matmul(ps[out_rows, 4 + u % 4, 0:n], lhs, rhs, start=True, stop=True)
                ins.then_inc(s("aux_done"), 1)

            full = slice(0, P)
            for n in range(10):
                proj(n)
            pe.wait_ge(s("aux_evac"), 1)
            pe.wait_ge(s("conv"), 1)
            pe.wait_ge(s("ld_lruw"), 64)
            for g in range(2):
                for j in range(4):
                    aux(1 + 4 * g + j, *[(slice(64 * h, 64 * h + 64), lruw[64 * h:64 * h + 64, g, j],
                                          xc[64 * h:64 * h + 64, j]) for h in range(2)])
            for n in range(10, 18):
                proj(n)
            pe.wait_ge(s("ld_lora"), 48)
            pe.wait_ge(s("lora_in"), 2)
            for g in range(2):
                r = slice(64 * g, 64 * g + 64)
                for j in range(4):
                    aux(9 + 4 * g + j, (full, lora[r, j * P:(j + 1) * P], WA[r, :]))
            for j in range(4):
                aux(17 + j, (full, gup[:, j * P:(j + 1) * P], GD[:, :]))
            proj(18)
            proj(19)
            pe.wait_ge(s("delta_in"), 1)
            pe.wait_ge(s("consts"), 2)
            for j in range(4):
                aux(21 + j, (full, onesbd[:, :], Bt[:, j]), n=TP)
            proj(20)
            proj(21)
            pe.wait_ge(s("delta_in"), 2)
            for j in range(4):
                aux(25 + j, (full, onesbd[:, :], KK[:, j]), n=TP)
            pe.wait_ge(s("delta_in"), 3)
            pe.wait_ge(s("aux_evac"), 29)
            for c in range(NC):
                t = slice(c * L, (c + 1) * L)
                if c >= 1:
                    pe.wait_ge(s("pm_evac"), c)
                    pe.wait_ge(s("tok_evac"), c)
                for j in range(4):
                    for h in range(2):
                        r = slice(64 * h, 64 * h + 64)
                        ar = AR[r, j, c].rearrange("p x t -> p (x t)")
                        pe.matmul(ps[r, 0, j * P:(j + 1) * P], Bt[r, j, t], ar, start=True, stop=True)
                        pe.matmul(ps[r, 1, j * P:(j + 1) * P], Kt[r, j, t], ar, start=True, stop=True)
                        pe.matmul(ps[r, 2, 256 + j * L:256 + (j + 1) * L], vT[r, j, t], id64[r, :], start=True, stop=True)
                        pe.matmul(ps[r, 3, j * L:(j + 1) * L], Kt[r, j, t], id64[r, :], start=True, stop=True)
                        ins = pe.matmul(ps[r, 3, 256 + j * L:256 + (j + 1) * L], Bt[r, j, t], id64[r, :],
                                        start=True, stop=True)
                ins.then_inc(s("pm_done"), 1)
            pe.wait_ge(s("pm_evac"), NC)
            for n in range(5 * NC):
                c = n % NC
                pe.wait_ge(s("x_set"), n + 1)
                if n >= 2:
                    pe.wait_ge(s("y_evac"), n - 1)
                for j in range(4):
                    for h in range(2):
                        r = slice(64 * h, 64 * h + 64)
                        ins = pe.matmul(ps[r, 4 + n % 2, j * L:(j + 1) * L], CT[r, c, j], X[r, c, j],
                                        start=True, stop=True)
                ins.then_inc(s("y_done"), 1)
                pe.wait_ge(s("y_evac"), n + 1)
                if n >= 2:
                    pe.wait_ge(s("z_used"), n - 1)
                for j in range(4):
                    for h in range(2):
                        r = slice(64 * h, 64 * h + 64)
                        lhs, rhs = (XT[r, c, j], YY[r, c, j]) if n < 4 * NC else (YY[r, c, j], XT[r, c, j])
                        ins = pe.matmul(ps[r, 6 + n % 2, j * L:(j + 1) * L], lhs, rhs, start=True, stop=True)
                ins.then_inc(s("z_done"), 1)
            pe.wait_ge(s("z_used"), 5 * NC)
            pe.wait_ge(s("pm_evac"), NC)
            pe.wait_ge(s("tok_evac"), NC)
            for c in range(NC):
                t = slice(c * L, (c + 1) * L)
                pe.wait_ge(s("st_set"), c + 1)

                def heads(bank, *terms, js=range(4)):
                    for j in js:
                        for i, (lhs, rhs) in enumerate(terms):
                            for h in range(2):
                                r = slice(64 * h, 64 * h + 64)
                                ins = pe.matmul(ps[r, bank, j * L:(j + 1) * L], lhs(r, j), rhs(r, j),
                                                start=(i == 0), stop=(i == len(terms) - 1))
                    return ins

                heads(0, (lambda r, j: AR[r, j, c, 0], lambda r, j: ST[r, j]),
                      (lambda r, j: MB[r, c, j, 0], lambda r, j: Vtk[r, c, j])).then_inc(s("rh_done"), 1)
                out_terms = ((lambda r, j: ST[r, j], lambda r, j: AR[r, j, c, 1]),
                             (lambda r, j: Vtk[r, c, j], lambda r, j: MB[r, c, j, 1]))
                if c >= 1:
                    pe.wait_ge(s("o_evac"), c)
                heads(2, *out_terms, js=(0, 1))
                pe.wait_ge(s("rh_evac"), c + 1)
                heads(1, (lambda r, j: XT[r, c, j], lambda r, j: RH[r, j])).then_inc(s("sa_done"), 1)
                heads(2, *out_terms, js=(2, 3)).then_inc(s("o_done"), 1)
                pe.wait_ge(s("sa_evac"), c + 1)
                heads(3, (lambda r, j: Ktk[r, c, j], lambda r, j: Vtk[r, c, j]),
                      (lambda r, j: Btk[r, c, j], lambda r, j: nSA[r, j])).then_inc(s("ds_done"), 1)
                if c >= 1:
                    pe.wait_ge(s("o_add"), c)
                heads(4, (lambda r, j: nSA[r, j], lambda r, j: MA[r, c, j, 1])).then_inc(s("osa_done"), 1)
            pe.wait_ge(s("o_add"), NC)
            for j in range(4):
                aux(29 + j, (full, onesbd[:, :], oT[:, j, PAD:TP]))
            for j in range(4):
                pe.wait_ge(s("o_sq"), j + 1)
                aux(33 + j, (full, onesbd[:, :], X.rearrange("p c j t -> p (c j t)").rearrange(
                    "p (j t) -> p j t", j=4)[:, j, PAD:TP]))

            def out_proj(y):
                pe.wait_ge(s("ld_wout"), 16 * (y + 1))
                pe.wait_ge(s("mix_ready"), y + 1)
                for m in range(KD):
                    if m >= 4:
                        pe.wait_ge(s("res_add"), KD * y + m - 3)
                    for k in range(8):
                        ins = pe.matmul(ps[:, m % 4, 0:T], wout[:, k, m::KD], mixT[:, k], start=(k == 0), stop=(k == 7))
                    ins.then_inc(s("res_done"), 1)

            def norm(i):
                for k in range(KD):
                    pe.wait_ge(s("nsq"), 8 * i + k - 7)
                    ins = pe.matmul(ps[:, 7, 0:T], ones[:, :], sq[:, k], start=(k == 0), stop=(k == KD - 1))
                ins.then_inc(s("nss"), 1)

            def experts(y):
                p0 = pe_passes[y - 1]
                norm(2 * y + 1)
                pe.wait_ge(s("xn"), KD * (2 * y + 1))
                pe.wait_ge(s("ld_wr"), 32 * (y + 1))
                for m in range(2):
                    for n, (t0, cnt) in enumerate(TILES):
                        half = min(64, cnt - 64 * m)
                        for k in range(KD if half > 0 else 0):
                            ins = pe.matmul(ps[64 * m:64 * m + half, 6, n * 36:n * 36 + 36],
                                            xnE[:, k, t0 + 64 * m:t0 + 64 * m + half], wr[:, k, :],
                                            start=(k == 0), stop=(k == KD - 1))
                ins.then_inc(s("lg_done"), 1)
                for n, (t0, cnt) in enumerate(TILES):
                    for k in range(KD):
                        ins = pe.transpose(ps[0:cnt, 2 * n + k // 4, (k % 4) * P:(k % 4) * P + P],
                                           xnE[:, k, t0:t0 + cnt], ident[:, :])
                    ins.then_inc(s("row_tr"), 1)
                pe.wait_ge(s("A_set"), y + 1)
                M = META
                terms = [[(before[:, :], AA[:, 0])],
                         [(ones[:, :], AA[:, 0]), (before[:, :], AA[:, 1])],
                         [(ones[:, :], AA[:, 0]), (ones[:, :], AA[:, 1]), (before[0:M, :], AA[0:M, 2])],
                         [(ones[:, :], AA[:, 0]), (ones[:, :], AA[:, 1]), (ones[0:M, :], AA[0:M, 2])]]
                for n, t in enumerate(terms):
                    for i, (lhs, rhs) in enumerate(t):
                        ins = pe.matmul(ps[:, 7, n * NE:(n + 1) * NE], lhs, rhs, start=(i == 0), stop=(i == len(t) - 1))
                ins.then_inc(s("rk_done"), 1)
                pe.wait_ge(s("npass"), y + 1)
                passes = pe_passes[y] = pe.value_load(np_i[0:1, y:y + 1], min_val=1, max_val=5)
                pe.wait_ge(s("part2"), 6 * y + 6)
                pe.wait_ge(s("part3"), 6 * y + 6)

                def gather(it, n, ks):
                    for k in ks:
                        o = ps[:, k // 2, (k % 2) * 256:(k % 2) * 256 + 256]
                        c = slice(k * P, (k + 1) * P)
                        for t in range(2):
                            for x in range(3):
                                pe.matmul(o, xpart[:, t, x, c], Rb[:, t], start=(t == 0 and x == 0), stop=False)
                        ins = pe.matmul(o, xmeta[:, c], Rm, start=False, stop=True)
                    if ks[-1] == KD - 1:
                        ins.then_inc(s("g_done"), 1)
                    else:
                        for b in range(2):
                            for t, cnt in ((0, P), (1, P), (2, META)):
                                lhs = Rb[:, t, b * P:(b + 1) * P] if t < 2 else Rm[0:META, b * P:(b + 1) * P]
                                ins = pe.matmul(ps[:, 5, 256 + 11 * b:267 + 11 * b], lhs, VV[0:cnt, t, bass.ds(2 * n + b, 1), 0:11]
                                                .rearrange("p a x -> p (a x)"), start=(t == 0), stop=(t == 2))
                        ins.then_inc(s("tb_done"), 1)

                def step(it, n, more):
                    for b in range(2):
                        i = 2 * it + b
                        w = slot_w[b]
                        if b == 0:
                            pe.wait_ge(s("xga"), it + 1)
                            pe.wait_ge(s("xgd"), it + 1)
                        pe.wait_ge(s(f"ld_gu{b}"), it * 32 + 32)
                        for k in range(KD):
                            for e in range(2):
                                r = slice(64 * e, 64 * e + 64)
                                gu = w[:, e, 0:4096].rearrange("p (x k f) -> p x k f", x=2, k=KD)
                                ins = pe.matmul(ps[r, 4, :], xgT[:, k, b * P + 64 * e:b * P + 64 * e + 64], gu[:, :, k, :],
                                                start=(k == 0), stop=(k == KD - 1))
                        ins.then_inc(s("gu_done"), 1)
                        if more:
                            if b == 0:
                                pe.wait_ge(s("R_set"), it + 2)
                            gather(it + 1, n + 1, range(4 * b, 4 * b + 4))
                        pe.wait_ge(s("hid"), i + 1)
                        if more and b == 0:
                            pe.wait_ge(s("tb_evac"), it + 2)
                        for k in range(2):
                            ins = pe.transpose(ps[:, 5, k * P:(k + 1) * P], hid[:, k::2], ident[:, :])
                        ins.then_inc(s("ht_done"), 1)
                        pe.wait_ge(s("hte"), i + 1)
                        pe.wait_ge(s(f"ld_d{b}"), it * 16 + 16)
                        pe.wait_ge(s("ya"), i + 1)
                        pe.wait_ge(s("yd"), i + 1)
                        for hf in range(2):
                            for k in range(2):
                                for e in range(2):
                                    r = slice(64 * e, 64 * e + 64)
                                    dn = w[:, e, 4096 + k * D + hf * 512:4096 + k * D + hf * 512 + 512]
                                    ins = pe.matmul(ps[r, 6 + hf, :], hidT[:, k, r], dn, start=(k == 0), stop=(k == 1))
                        ins.then_inc(s("rows_done"), 1)

                with pe.Fori(0, passes) as q:
                    pe.wait_ge(s("R_set"), (q + p0) * NIT + 1)
                    gather((q + p0) * NIT, 0, range(0, 4))
                    gather((q + p0) * NIT, 0, range(4, 8))
                    with pe.Fori(0, NIT - 1) as n:
                        step((q + p0) * NIT + n, n, True)
                    step((q + p0) * NIT + NIT - 1, NIT - 1, False)
                pe.sem_inc(s("pe_end"), 1)
                if y == 0:
                    for n, (t0, cnt) in enumerate(TILES):
                        pe.wait_ge(s("y_sum"), n + 1)
                        for k in range(KD):
                            bk = 2 * n + k // 4 if n < 2 else 4
                            o = ps[:, bk, (k % 4) * P:(k % 4) * P + cnt] if n < 2 else ps[:, bk, k * META:(k + 1) * META]
                            ins = pe.transpose(o, yrow[0:cnt, n, 0, k::KD], ident[0:cnt, 0:cnt])
                            if k % 4 == 3 and (n < 2 or k == 7):
                                ins.then_inc(s("h_tr"), 1)
                else:
                    pe.wait_ge(s("y_sum"), 4)
                    for n, (t0, cnt) in enumerate(TILES[:2]):
                        for k in range(KD):
                            ins = pe.transpose(ps[:, 2 * n + k // 4, (k % 4) * P:(k % 4) * P + P],
                                               hT[:, k, t0:t0 + P], ident[:, :])
                        ins.then_inc(s("hr_done"), 1)

            out_proj(0)
            experts(0)
            norm(2)
            pe.wait_ge(s("ld_gupO"), 16)
            pe.wait_ge(s("xn"), 2 * KD)
            unit = 0

            def decayed_rows():
                pe.wait_ge(s("kd_set"), 1)
                pe.wait_ge(s("gx_evac"), 4)
                for h in range(4):
                    for c in range(NC):
                        sl, half = PLACE[c]
                        ins = pe.matmul(ps[64 * half:64 * half + 64, 4 + sl, h * P:(h + 1) * P],
                                        KDc[:, h, c * L:(c + 1) * L], ident[:, :], start=True, stop=True)
                ins.then_inc(s("kdt_done"), 1)

            def pairs(i):
                if i > 0:
                    pe.wait_ge(s("qk_set"), i)
                if i < 2:
                    pe.wait_ge(s("kdt_set"), 1)
                else:
                    pe.wait_ge(s("pt_used"), i - 1)
                qq, kk = (qO, kO) if i == 0 else (QH, KH)
                for h in range(4):
                    for c in (1, 2, 3, 4, 0):
                        sl, half = PLACE[c]
                        bk, o = (4 + 2 * (i % 2), sl * 256) if sl < 2 else (5 + 2 * (i % 2), 0)
                        ins = pe.matmul(ps[64 * half:64 * half + 64, bk, o + h * L:o + (h + 1) * L],
                                        kk[:, h, c * L:(c + 1) * L], qq[:, h, c * L:(c + 1) * L], start=True, stop=True)
                ins.then_inc(s("pt_done"), 1)

            for g, (c0, w) in enumerate(O_GROUPS):
                pe.wait_ge(s(f"ld_w{g % 6}"), 16 * (g // 6 + 1 + (2 if g % 6 < 5 else 1)))
                wg = wring[:, g % 6]
                if g == 0:
                    todo = [(slice(0, 16), T, lambda k: wg[:, k, 0:16], lambda k: xnO[:, k, PAD:TP])]
                elif 5 <= g < 9:
                    todo = [(slice(0, cnt), 256, lambda k, c=c0_, n=cnt: xnO[:, k, c:c + n], lambda k: wg[:, k, :])
                            for c0_, cnt in ((L, P), (3 * L, P), (0, L))]
                else:
                    todo = [(slice(0, P), T, lambda k, m=m: wg[:, k, m * P:(m + 1) * P], lambda k: xnO[:, k, PAD:TP])
                            for m in range(2)]
                for rows, n, lhs, rhs in todo:
                    if unit >= 4:
                        pe.wait_ge(s("oproj_evac"), unit - 3)
                    for k in range(KD):
                        ins = pe.matmul(ps[rows, unit % 4, 0:n], lhs(k), rhs(k), start=(k == 0), stop=(k == KD - 1))
                    ins.then_inc(s("oproj"), 1)
                    unit += 1
                    if unit == 14:
                        decayed_rows()
                    if unit >= 15 and unit % 2 == 1 and unit < 29:
                        pairs((unit - 15) // 2)
                if g == 4:
                    for j in range(4):
                        pe.matmul(ps[:, 4 + j, 0:T], gupO[:, j * P:(j + 1) * P], gdT, start=True, stop=True) \
                            .then_inc(s("gx"), 1)
            pe.wait_ge(s("oproj_evac"), 29)
            pe.wait_ge(s("pt_used"), 7)
            pe.wait_ge(s("kdt_set"), 1)

            def state_in(c):
                sl, half = PLACE[c]
                r = slice(64 * half, 64 * half + 64)
                for h in range(4):
                    ins = pe.matmul(ps[:, 2 + 2 * (c % 3) + h // 2, (h % 2) * 256:(h % 2) * 256 + 256], kdt[r, sl, h, :],
                                    Vo[r, sl, h * 256:(h + 1) * 256], start=True, stop=True)
                ins.then_inc(s("sg_done"), 1)

            for c in range(3):
                state_in(c)
            for c in range(NC):
                sl, half = PLACE[c]
                r = slice(64 * half, 64 * half + 64)
                pe.wait_ge(s("sg_set"), 4 * c + 1)
                if c >= 2:
                    pe.wait_ge(s("og_evac"), c - 1)
                for m in range(2):
                    for h in range(4):
                        for x in range(2):
                            o = ps[64 * m:64 * m + 64, c % 2, (2 * h + x) * L:(2 * h + x + 1) * L]
                            v0 = x * P + 64 * m
                            pe.matmul(o, SG[c % 2][:, h, v0:v0 + 64], QE[:, h, c * L:(c + 1) * L], start=True, stop=False)
                            ins = pe.matmul(o, Vo[r, sl, h * 256 + v0:h * 256 + v0 + 64], PT[r, sl, h, :],
                                            start=False, stop=True)
                ins.then_inc(s("og_done"), 1)
                if c == 1:
                    state_in(3)
            for h in range(4):
                for x in range(2):
                    pe.wait_ge(s("og_sq"), 2 * h + x + 1)
                    ins = pe.matmul(ps[:, 4 + h, 0:T], ones[:, :], sqG[:, 2 * h + x], start=(x == 0), stop=(x == 1))
                ins.then_inc(s("og_ss"), 1)
            out_proj(1)
            experts(1)

        @block.vector
        def _(v):
            v_passes = {-1: 0}
            n_link = [0]

            def link(ins):
                n_link[0] += 1
                ins.then_inc(s("dve_chain"), 1)
                v.wait_ge(s("dve_chain"), n_link[0])

            def col(name, j):
                return pv[:, PV[name] + j:PV[name] + j + 1]

            tt = v.tensor_tensor
            stt = v.scalar_tensor_tensor
            v.memset(epsb[:, 0:1], EPS)
            v.memset(epsb[:, 1:2], GN_EPS).then_inc(s("eps_set"), 1)
            for i in range(5):
                v.wait_ge(s("h_tr"), i + 1)
                if i < 4:
                    t0 = TILES[i // 2][0]
                    k0 = 4 * (i % 2)
                    v.tensor_copy(hT[:, k0:k0 + 4, t0:t0 + P], ps[:, i, :].rearrange("p (k t) -> p k t", k=4)) \
                        .then_inc(s("h_ready"), 1)
                else:
                    v.tensor_copy(hT[:, :, 0:META], ps[:, 4, 0:P].rearrange("p (k t) -> p k t", k=8)) \
                        .then_inc(s("h_ready"), 1)
            v.wait_ge(s("pv_tr"), 1)
            v.tensor_copy(pv[:, :], ps[:, 5, 0:NPV]).then_inc(s("pv_set"), 1)
            v.wait_ge(s("pv_set"), 1)
            lam = pv[:, PV["lam"]:PV["lam"] + 4]
            link(v.tensor_scalar(slam[:, 2], lam, -1.0, None, ALU.mult))
            tt(slam[:, 0], lam, slam[:, 2], ALU.max).then_inc(s("lam_abs"), 1)
            link(v.tensor_scalar(omka[:, :], pv[:, PV["k_a"]:PV["k_a"] + 4], -1.0, 1.0, ALU.mult, ALU.add))
            v.wait_ge(s("aux_evac"), 1)
            v.wait_ge(s("ld_gain"), 64)
            link(v.reciprocal(rs, rs))
            for k in range(KD):
                stt(out=xnE[:, k], in0=hT[:, k], scalar=gains[:, 0, k:k + 1], in1=rs, op0=ALU.mult, op1=ALU.mult) \
                    .then_inc(s("xn0"), 1)
            v.wait_ge(s("xn0"), KD)
            v.memset(xb[:, :, 0:3], 0.0)
            v.memset(raw[:, :, 0:1], 0.0)
            for x in (rT, kT, vT, aT, EX):
                if x is not EX:
                    v.memset(x[:, :, 0:PAD], 0.0)
            v.memset(reset[:, :], 1.0)
            link(v.memset(EX[:, :, 0:PAD], 0.0))
            link(v.memset(reset[:, :].rearrange("p (c t) -> p c t", t=L)[:, :, 0], 0.0))
            v.sem_inc(s("pads_zero"), 1)
            v.wait_ge(s("lam_exp"), 1)
            link(v.tensor_scalar(slam[:, 3], slam[:, 1], 2.0, None, ALU.add))
            link(v.reciprocal(slam[:, 3], slam[:, 3]))
            link(tt(slam[:, 3], slam[:, 3], slam[:, 1], ALU.mult))
            link(tt(slam[:, 4], slam[:, 3], slam[:, 3], ALU.mult))
            link(v.memset(slam[:, 5], 1.0 / 17))
            for i in range(7, -1, -1):
                link(tt(slam[:, 5], slam[:, 5], slam[:, 4], ALU.mult))
                link(v.tensor_scalar(slam[:, 5], slam[:, 5], 1.0 / (2 * i + 1), None, ALU.add))
            link(tt(slam[:, 5], slam[:, 5], slam[:, 3], ALU.mult))
            link(v.tensor_scalar(slam[:, 2], slam[:, 2], 0.0, None, ALU.max))
            link(stt(out=slam[:, 5], in0=slam[:, 5], scalar=2.0, in1=slam[:, 2], op0=ALU.mult, op1=ALU.add))
            v.tensor_scalar(slam[:, 5], slam[:, 5], -8.0, None, ALU.mult).then_inc(s("slam_set"), 1)
            v.wait_ge(s("proj_evac"), 4)
            for j in range(4):
                cw = [pv[:, PV["conv_w"] + 4 * i + j:PV["conv_w"] + 4 * i + j + 1] for i in range(4)]
                link(v.tensor_scalar(xc[:, j], xb[:, j, 3:T + 3], cw[3], col("conv_b", j), ALU.mult, ALU.add))
                for i in range(3):
                    link(stt(out=xc[:, j], in0=xb[:, j, i:i + T], scalar=cw[i], in1=xc[:, j], op0=ALU.mult, op1=ALU.add))
            v.sem_inc(s("conv"), 1)
            v.wait_ge(s("proj_evac"), 8)
            link(tt(t2, gb, gb, ALU.mult))
            link(v.tensor_scalar(t2, t2, 0.044715, 1.0, ALU.mult, ALU.add))
            tt(t2, t2, gb, ALU.mult).then_inc(s("lru_in"), 1)

            def shift(i, dst, m):
                v.wait_ge(s("proj_evac"), 9 + i)
                q = raw[:, i % 4]
                link(tt(DT, q[:, 0:T], q[:, 1:T + 1], ALU.subtract))
                stt(out=dst, in0=DT, scalar=col("mu", m), in1=q[:, 1:T + 1], op0=ALU.mult, op1=ALU.add) \
                    .then_inc(s("shifted"), 1)
                v.wait_ge(s("shifted"), i + 1)

            shift(0, WA, 12)
            shift(1, GD, 13)
            shift(2, kT[:, 0, PAD:TP], 4)
            v.wait_ge(s("lru_a"), 8)
            link(tt(xb[:, :, 0:T], aa, aa, ALU.mult))
            stt(out=t1, in0=xb[:, :, 0:T], scalar=1.0, in1=t1, op0=ALU.add, op1=ALU.mult).then_inc(s("lru_in"), 1)
            shift(3, kT[:, 1, PAD:TP], 5)
            v.wait_ge(s("lru_a"), 9)
            link(stt(out=t2, in0=t2, scalar=1.0, in1=gb, op0=ALU.add, op1=ALU.mult))
            link(tt(gi, gi, xc, ALU.mult))
            shift(4, kT[:, 2, PAD:TP], 6)
            v.wait_ge(s("lru_a"), 10)
            link(tt(gi, gi, t1, ALU.mult))
            for j in range(4):
                last = v.tensor_tensor_scan(hh[:, j], aa[:, j], gi[:, j], 0.0, ALU.mult, ALU.add)
            link(last)
            shift(5, kT[:, 3, PAD:TP], 7)
            link(stt(out=mixT[:, 4:8], in0=hh, scalar=0.5, in1=t2, op0=ALU.mult, op1=ALU.mult))
            for j in range(4):
                shift(6 + j, rT[:, j, PAD:TP], j)
            for j in range(4):
                last = v.tensor_scalar(KK[:, j], kT[:, j], col("k_k", j), None, ALU.mult)
            link(last)
            tt(Bt, KK, KK, ALU.mult).then_inc(s("delta_in"), 1)
            v.wait_ge(s("aux_evac"), 17)
            link(v.tensor_scalar(LW, EX, -0.6065306597126334, None, ALU.mult))
            link(v.tensor_tensor_scan(CUM.rearrange("p j t -> p (j t)"), reset[:, :], LW.rearrange("p j t -> p (j t)"),
                                      0.0, ALU.mult, ALU.add))
            tt(LW, CUM, LW, ALU.subtract).then_inc(s("cum_set"), 1)
            ar = AR.rearrange("p j c x t -> p (j c) x t")

            def ch(x):
                return x.rearrange("p j (c t) -> p (j c) t", t=L)

            for j in range(2):
                shift(10 + j, vT[:, j, PAD:TP], 8 + j)
            v.wait_ge(s("aux_evac"), 25)
            link(v.tensor_scalar(Kt, Kt, 1e-12, None, ALU.max))
            link(v.reciprocal(Kt, Kt))
            link(tt(KK, KK, Kt, ALU.mult))
            v.wait_ge(s("exps"), 1)
            tt(ar[:, :, 0], ch(KK), ch(EX), ALU.mult).then_inc(s("ex_used"), 1)
            for j in range(4):
                last = v.tensor_scalar(KM[:, j], aT[:, j], col("k_a", j), omka[:, j:j + 1], ALU.mult, ALU.add)
            link(last)
            link(tt(KM, KM, kT, ALU.mult))
            link(tt(Bt, KK, aT, ALU.mult))
            shift(12, vT[:, 2, PAD:TP], 10)
            v.wait_ge(s("exps"), 2)
            v.tensor_copy(dlast[:, :, :], EX.rearrange("p j (c t) -> p j c t", t=L)[:, :, :, L - 1])
            tt(ar[:, :, 1], ch(rT), ch(EX), ALU.mult).then_inc(s("ex_used"), 1)
            shift(13, vT[:, 3, PAD:TP], 11)
            for j in range(4):
                last = stt(out=KK[:, j], in0=rT[:, j], scalar=col("r_k", j), in1=KM[:, j], op0=ALU.mult, op1=ALU.mult)
            last.then_inc(s("delta_in"), 1)
            v.wait_ge(s("exps"), 3)
            tt(Kt, KM, EX, ALU.mult)
            tt(Bt, Bt, EX, ALU.mult).then_inc(s("delta_in"), 1)
            v.wait_ge(s("aux_evac"), 29)
            link(tt(BV, BV, vT, ALU.mult))
            def over(m, n):
                return m[:, None, :].to_broadcast([P, n, m.shape[-1]]) if len(m.shape) == 2 else None

            v.wait_ge(s("consts"), 2)
            for c in range(NC):
                v.wait_ge(s("pm_done"), c + 1)
                mar = m_ar[:, :, :].rearrange("p x t -> p (x t)").unsqueeze(1).to_broadcast([P, 4, 2 * L])
                tt(MA[:, c].rearrange("p j x t -> p j (x t)"), ps[:, 0, :].rearrange("p (j y) -> p j y", j=4), mar, ALU.mult)
                tt(MB[:, c].rearrange("p j x t -> p j (x t)"), ps[:, 1, :].rearrange("p (j y) -> p j y", j=4), mar,
                   ALU.mult).then_inc(s("pm_evac"), 1)
            v.wait_ge(s("pm_evac"), NC)
            nt = MA.rearrange("p c j x t -> p (c j) x t")[:, :, 0]
            xx, xt = X.rearrange("p c j t -> p (c j) t"), XT.rearrange("p c j t -> p (c j) t")

            def wide(m):
                return m.unsqueeze(1).to_broadcast([P, 4 * NC, L])

            link(v.tensor_tensor(xt, nt, wide(m_lev[:, 0]), ALU.mult))
            link(tt(xt, wide(id64[:, :]), xt, ALU.subtract))
            v.transpose(X.rearrange("p c j t -> p (c j t)"), XT.rearrange("p c j t -> p (c j t)"))

            def couple(lev, c):
                return tt(CT[:, c], MA[:, c, :, 0], m_lev[:, lev].unsqueeze(1).to_broadcast([P, 4, L]), ALU.mult)

            for c in range(NC):
                couple(1, c).then_inc(s("x_set"), 1)
            for n in range(5 * NC):
                lev, c = n // NC + 1, n % NC
                v.wait_ge(s("z_done"), n + 1)
                z = ps[:, 6 + n % 2, 0:256].rearrange("p (j t) -> p j t", j=4)
                if lev < 5:
                    tt(X[:, c], X[:, c], z, ALU.subtract)
                    couple(lev + 1, c).then_inc(s("x_set"), 1)
                    v.wait_ge(s("x_set"), NC + n + 1)
                    v.transpose(XT[:, c].rearrange("p j t -> p (j t)"), X[:, c].rearrange("p j t -> p (j t)")) \
                        .then_inc(s("z_used"), 1)
                else:
                    tt(XT[:, c], XT[:, c], z, ALU.subtract).then_inc(s("z_used"), 1)
            v.wait_ge(s("pm_done"), NC)
            v.memset(ST, 0.0).then_inc(s("st_set"), 1)
            for c in range(NC):
                v.wait_ge(s("ds_done"), c + 1)
                v.wait_ge(s("st_set"), c + 1)
                link(tt(STn, ST, ps[:, 3, 0:256].rearrange("p (j v) -> p j v", j=4), ALU.add))
                v.wait_ge(s("o_done"), c + 1)
                tt(ST, STn, dlast[:, :, c:c + 1].to_broadcast([P, 4, L]), ALU.mult).then_inc(s("st_set"), 1)
                v.wait_ge(s("o_evac"), c + 1)
                v.wait_ge(s("osa_done"), c + 1)
                oc = oT[:, :, c * L:(c + 1) * L]
                tt(oc, oc, ps[:, 4, 0:256].rearrange("p (j t) -> p j t", j=4), ALU.add).then_inc(s("o_add"), 1)
            oq = X.rearrange("p c j t -> p (c j t)").rearrange("p (j t) -> p j t", j=4)
            mean, root = LW, CUM
            for j in range(4):
                v.wait_ge(s("aux_evac"), 30 + j)
                v.wait_ge(s("o_add"), NC)
                link(tt(oT[:, j, PAD:TP], oT[:, j, PAD:TP], mean[:, j, 0:T], ALU.subtract))
                tt(oq[:, j, PAD:TP], oT[:, j, PAD:TP], oT[:, j, PAD:TP], ALU.mult).then_inc(s("o_sq"), 1)
            for j in range(4):
                v.wait_ge(s("aux_evac"), 34 + j)
                link(v.reciprocal(root[:, j, 0:T], root[:, j, 0:T]))
                link(tt(oT[:, j, PAD:TP], oT[:, j, PAD:TP], root[:, j, 0:T], ALU.mult))
                link(v.tensor_scalar(oT[:, j, PAD:TP], oT[:, j, PAD:TP], col("ln_g", j), col("ln_b", j), ALU.mult, ALU.add))
                link(tt(oT[:, j, PAD:TP], oT[:, j, PAD:TP], BV[:, j, PAD:TP], ALU.add))
                ins = tt(mixT[:, j], oT[:, j, PAD:TP], GT[:, j, PAD:TP], ALU.mult)
            ins.then_inc(s("mix_ready"), 1)

            link(v.tensor_scalar(tok_l[:, :], tok_i[:, :], 15, None, ALU.bitwise_and))
            link(v.tensor_copy(tokp[:, 0], tok_i[:, :]))
            link(v.tensor_copy(tokp[:, 1], tok_l[:, :]))
            link(tt(tokp[:, 0], tokp[:, 0], tokp[:, 1], ALU.subtract))
            v.sem_inc(s("yd"), 1)

            def res_add(y):
                for m in range(KD):
                    v.wait_ge(s("res_done"), KD * y + m + 1)
                    tt(hT[:, m], hT[:, m], ps[:, m % 4, 0:T], ALU.add).then_inc(s("res_add"), 1)
                v.wait_ge(s("res_add"), KD * (y + 1))

            def norm(i, gain, scratch, dst):
                v.wait_ge(s("nrs"), i)
                link(v.reciprocal(scratch, scratch))
                for k in range(KD):
                    stt(out=dst[:, k], in0=hT[:, k], scalar=gains[:, gain, k:k + 1], in1=scratch,
                        op0=ALU.mult, op1=ALU.mult).then_inc(s("xn"), 1)

            def wide3(x, n):
                return x.unsqueeze(2).to_broadcast([P, 3, n])

            def first_max(dst, src, top, n, tmp):
                link(tt(tmp, src, wide3(top, n), ALU.is_equal))
                link(tt(tmp, tmp, rev[:, 8 - n:].unsqueeze(1).to_broadcast([P, 3, n]), ALU.mult))
                link(v.tensor_reduce(gsum, tmp, AXX, ALU.max))
                link(tt(dst, tmp, wide3(gsum, n), ALU.is_equal))

            def experts(y):
                p0 = v_passes[y - 1]
                v.memset(xmeta, 0.0).then_inc(s("xm_set"), 1)
                norm(2 * y + 1, 2 + y, rsM, xnE)
                v.wait_ge(s("lg_done"), y + 1)
                v.wait_ge(s("ld_bi"), 32 * (y + 1))
                link(v.memset(LG, 0.0))
                for n, (_, cnt) in enumerate(TILES):
                    ins = tt(LG[0:cnt, n], ps[0:cnt, 6, n * 36:n * 36 + 36], BI[0:cnt, :], ALU.add)
                link(ins)
                link(v.tensor_reduce(gmax, LG[:, :, 0:NG], AXX, ALU.max))
                tt(eg, LG[:, :, 0:NG], wide3(gmax, NG), ALU.subtract).then_inc(s("route_in"), 1)
                first_max(ohg, LG[:, :, 0:NG], gmax, NG, sg4)
                link(tt(pe4, LG[:, :, NG:].rearrange("p t (g e) -> p t g e", g=NG),
                        ohg.unsqueeze(3).to_broadcast([P, 3, NG, 8]), ALU.mult))
                link(v.tensor_reduce(el, pe4.rearrange("p t g e -> p t e g"), AXX, ALU.add))
                link(v.tensor_reduce(v1, el, AXX, ALU.max))
                first_max(oh1, el, v1, 8, s8)
                link(stt(out=el, in0=oh1, scalar=-3e38, in1=el, op0=ALU.mult, op1=ALU.add))
                link(v.tensor_reduce(v2, el, AXX, ALU.max))
                tt(w2, v2, v1, ALU.subtract).then_inc(s("route_in"), 1)
                first_max(oh2, el, v2, 8, s8)
                v.wait_ge(s("route_exp"), 2 * y + 1)
                link(v.tensor_reduce(gsum, eg, AXX, ALU.add))
                v.wait_ge(s("route_exp"), 2 * y + 2)
                link(v.tensor_scalar(w1, w2, 1.0, None, ALU.add))
                link(tt(w1, w1, gsum, ALU.mult))
                link(v.reciprocal(w1, w1))
                link(tt(w2, w2, w1, ALU.mult))
                for o, oh in ((O1, oh1), (O2, oh2)):
                    for g in range(NG):
                        ins = tt(o[:, :, 8 * g:8 * g + 8], oh, ohg[:, :, g:g + 1].to_broadcast([P, 3, 8]), ALU.mult)
                link(ins)
                tt(AA, O1, O2, ALU.add).then_inc(s("A_set"), 1)
                link(tt(WT, O1, wide3(w1, NE), ALU.mult))
                link(tt(pe4.rearrange("p t g e -> p t (g e)"), O2, wide3(w2, NE), ALU.mult))
                link(tt(WT, WT, pe4.rearrange("p t g e -> p t (g e)"), ALU.add))
                pw = pe4.rearrange("p t g e -> p t (g e)")
                cols = VV.rearrange("p t i x -> p (t i) x")
                wt = WT.rearrange("p t (i x) -> p (t i) x", x=2)
                w4 = pw.rearrange("p t (i x) -> p (t i) x", x=2)
                o2 = O2.rearrange("p t (i x) -> p (t i) x", x=2)
                for n in range(3):
                    v.tensor_scalar(VV[:, n, :, 0], O2[:, n, 0:NPAIR], 0.0, tokp[:, 0, n:n + 1], ALU.mult, ALU.add)
                    v.tensor_scalar(VV[:, n, :, 1], O2[:, n, 0:NPAIR], 0.0, tokp[:, 1, n:n + 1], ALU.mult, ALU.add)
                v.memset(VV[:, :, :, 2], 1.0)
                for x in range(2):
                    v.tensor_copy(cols[:, :, 3 + 4 * x], o2[:, :, x])
                    link(v.tensor_copy(cols[:, :, 4 + 4 * x], wt[:, :, x]))
                    link(tt(w4[:, :, x], wt[:, :, x], cols[:, :, 4 + 4 * x], ALU.subtract))
                    link(v.tensor_copy(cols[:, :, 5 + 4 * x], w4[:, :, x]))
                    link(tt(cols[:, :, 6 + 4 * x], w4[:, :, x], cols[:, :, 5 + 4 * x], ALU.subtract))
                v.wait_ge(s("rk_done"), y + 1)
                link(v.tensor_reduce(cmx, ps[:, 7, 96:128], AXX, ALU.max))
                link(stt(out=RM, in0=ps[:, 7, 0:96].rearrange("p (t e) -> p t e", t=3), scalar=1.0, in1=AA,
                         op0=ALU.add, op1=ALU.mult))
                link(v.tensor_scalar(RM, RM, -1.0, None, ALU.add))
                link(v.memset(RMx, -1.0))
                for x in range(3):
                    ins = v.tensor_copy(RMx[32 * x:32 * x + META], RM[0:META, 2])
                link(ins)
                link(v.tensor_scalar(cmp5, lims[:, :], cmx, None, ALU.is_lt))
                link(v.tensor_reduce(cmx, cmp5, AXX, ALU.add))
                v.tensor_copy(np_i[:, y:y + 1], cmx).then_inc(s("npass"), 1)
                v.wait_ge(s("npass"), y + 1)
                passes = v_passes[y] = v.value_load(np_i[0:1, y:y + 1], min_val=1, max_val=5)

                def onehot(n):
                    for t in range(2):
                        tt(Rb[:, t].rearrange("p (e c) -> p e c", e=4), iota_b[:, :].unsqueeze(1).to_broadcast([P, 4, SLOTS]),
                           RM[:, t, bass.ds(4 * n, 4)].unsqueeze(2).to_broadcast([P, 4, SLOTS]), ALU.is_equal)
                    tt(Rm.rearrange("p (e c) -> p e c", e=4), iota_b[0:96, :].unsqueeze(1).to_broadcast([96, 4, SLOTS]),
                       RMx[0:96, bass.ds(4 * n, 4)].unsqueeze(2).to_broadcast([96, 4, SLOTS]), ALU.is_equal) \
                        .then_inc(s("R_set"), 1)

                def gathered(it):
                    v.wait_ge(s("g_done"), it + 1)
                    for b in range(2):
                        ins = v.tensor_copy(xgT[:, 4 + 2 * b:6 + 2 * b], ps[:, 2 + b, :].rearrange("p (k t) -> p k t", k=2))
                    ins.then_inc(s("xgd"), 1)

                def tables(it):
                    v.wait_ge(s("tb_evac"), it + 1)
                    for h in range(2):
                        r = slice(64 * h, 64 * h + 64)
                        v.tensor_copy(sel[r], tbs[r, :, 3 + 4 * h:7 + 4 * h])
                    tt(ix, tbs[:, :, 0], tbs[:, :, 1], ALU.add).then_inc(s("tbl"), 1)
                    v.wait_ge(s("tbl"), it * 6 + 1)
                    stt(out=ix, in0=tbs[:, :, 2], scalar=-FAR, in1=ix, op0=ALU.mult, op1=ALU.add).then_inc(s("tbl"), 1)
                    v.wait_ge(s("tbl"), it * 6 + 2)
                    stt(out=ix, in0=sel[:, :, 0], scalar=float(T), in1=ix, op0=ALU.mult, op1=ALU.add).then_inc(s("tbl"), 1)
                    v.tensor_reduce(wnext, sel[:, :, 1:4], AXX, ALU.add)
                    v.wait_ge(s("tbl"), it * 6 + 3)
                    v.tensor_scalar(ix, ix, FAR, None, ALU.add).then_inc(s("tbl"), 1)
                    v.wait_ge(s("tbl"), it * 6 + 4)
                    v.tensor_copy(inext, ix).then_inc(s("tbl"), 1)

                def step(it, n, more):
                    if more:
                        v.wait_ge(s("g_done"), it + 1)
                        onehot(n + 1)
                    for b in range(2):
                        v.wait_ge(s(f"y_free{b}"), it + 1)
                        if b == 0:
                            v.wait_ge(s("tbl"), it * 6 + 5)
                        v.tensor_copy(icur[:, b:b + 1], inext[:, b:b + 1])
                        v.tensor_copy(wcur[:, b:b + 1], wnext[:, b:b + 1]).then_inc(s("idx_set"), 1)
                    v.wait_ge(s("idx_set"), 2 * it + 2)
                    v.tensor_copy(ix, ix).then_inc(s("tbl"), 1)
                    for b in range(2):
                        i = 2 * it + b
                        v.wait_ge(s("sil"), i + 1)
                        tt(hid, sil, ps[:, 4, FF:2 * FF], ALU.mult).then_inc(s("hid"), 1)
                        if b == 1 and more:
                            gathered(it + 1)
                        if b == 0 and more:
                            v.wait_ge(s("tbl"), it * 6 + 6)
                            tables(it + 1)
                        v.wait_ge(s("rows_done"), i + 3)
                        v.tensor_scalar(yst[:, b, 512:1024], ps[:, 7, :], wcur[:, b:b + 1], None, ALU.mult) \
                            .then_inc(s("yd"), 1)

                with v.Fori(0, passes) as q:
                    onehot(0)
                    tables((q + p0) * NIT)
                    gathered((q + p0) * NIT)
                    with v.Fori(0, NIT - 1) as n:
                        step((q + p0) * NIT + n, n, True)
                    step((q + p0) * NIT + NIT - 1, NIT - 1, False)
                    v.tensor_scalar(RM, RM, float(-SLOTS), None, ALU.add)
                    v.tensor_scalar(RMx, RMx, float(-SLOTS), None, ALU.add).then_inc(s("rank_set"), 1)
                    v.wait_ge(s("rank_set"), q + p0 + 1)
                for n, (t0, cnt) in enumerate(TILES):
                    if y == 1 and n == 2:
                        v.wait_ge(s(f"ld_y{n}"), 32 * (y + 1))
                        continue
                    v.wait_ge(s(f"ld_y{n}"), 32 * (y + 1))
                    tt(yrow[0:cnt, n, 0], yrow[0:cnt, n, 0], yrow[0:cnt, n, 1], ALU.add) \
                        .then_inc(s("y_sum"), 1)

            res_add(0)
            experts(0)
            for i in range(5):
                v.wait_ge(s("h_tr"), i + 6)
                if i < 4:
                    t0 = TILES[i // 2][0]
                    k0 = 4 * (i % 2)
                    dst, src = hT[:, k0:k0 + 4, t0:t0 + P], ps[:, i, :].rearrange("p (k t) -> p k t", k=4)
                else:
                    dst, src = hT[:, :, 0:META], ps[:, 4, 0:P].rearrange("p (k t) -> p k t", k=8)
                tt(dst, dst, src, ALU.add).then_inc(s("h_ready"), 1)
            v.wait_ge(s("nss"), 2)
            v.memset(xnO[:, :, 0:PAD], 0.0)
            norm(2, 1, rsO, xnO[:, :, PAD:TP])
            for x in (qO, kO, EA):
                v.memset(x[:, :, 0:PAD], 0.0)
            link(v.memset(LA[:, :, 0:PAD], 0.0))
            link(v.memset(QH, 0.0))
            link(v.memset(KH, 0.0))
            v.sem_inc(s("opads"), 1)
            v.wait_ge(s("gln"), 1)
            link(v.tensor_scalar(LA, LA, 0.0, None, ALU.min))
            link(tt(LA, LA, EA, ALU.subtract))
            link(v.tensor_scalar(LA, LA, 1.0 / 16, None, ALU.mult))
            flat = lambda x: x.rearrange("p j t -> p (j t)")
            v.tensor_tensor_scan(flat(CU), reset[:, :], flat(LA), 0.0, ALU.mult, ALU.add).then_inc(s("cu_set"), 1)
            v.wait_ge(s("cu_set"), 1)
            cc = CU.rearrange("p j (c t) -> p (j c) t", t=L)
            tt(EA.rearrange("p j (c t) -> p (j c) t", t=L), cc[:, :, L - 1:L].to_broadcast([P, 4 * NC, L]), cc,
               ALU.subtract).then_inc(s("kd_in"), 1)
            v.wait_ge(s("oproj_evac"), 9)
            v.wait_ge(s("ge"), 1)
            v.tensor_copy(elast[:, :, :], EB.rearrange("p j (c t) -> p j c t", t=L)[:, :, :, L - 1])
            link(tt(QE, qO, EB, ALU.mult))
            v.wait_ge(s("ge"), 2)
            tt(KDc, kO, EA, ALU.mult).then_inc(s("kd_set"), 1)
            v.wait_ge(s("kd_set"), 1)

            def halves(x, m):
                return flat(x).rearrange("p (b x r) -> p b x r", x=2, r=m)

            def level_in(i):
                m = L >> (i + 1)
                nb = SLAB // (2 * m)
                e, c = halves((EB, EA)[i % 2], m), halves(CU, m)
                ref = c[:, :, 0, m - 1:m].to_broadcast([P, nb, m])
                tt(e[:, :, 0], ref, c[:, :, 0], ALU.subtract)
                tt(e[:, :, 1], c[:, :, 1], ref, ALU.subtract).then_inc(s("lev_in"), 1)

            def pt_add(i):
                v.wait_ge(s("pt_done"), i + 1)
                mask = id64[:, :] if i == 0 else m_lev[:, 6 - i]
                for rows, sl, bk, n in ((slice(0, P), slice(0, 2), 4 + 2 * (i % 2), 8),
                                        (slice(0, 64), slice(2, 3), 5 + 2 * (i % 2), 4)):
                    dst = (PT if i == 0 else PTt)[rows, sl].rearrange("p s h t -> p (s h) t")
                    mk = mask[rows].unsqueeze(1).to_broadcast([rows.stop, n, L])
                    ins = tt(dst, ps[rows, bk, 0:n * L].rearrange("p (x t) -> p x t", t=L), mk, ALU.mult)
                ins.then_inc(s("pt_used"), 1)
                v.wait_ge(s("pt_used"), i + 1)
                if i:
                    tt(PT[:, 0:2], PT[:, 0:2], PTt[:, 0:2], ALU.add)
                    link(tt(PT[0:64, 2], PT[0:64, 2], PTt[0:64, 2], ALU.add))

            level_in(0)
            for i in range(6):
                m = L >> (i + 1)
                if i < 5:
                    level_in(i + 1)
                v.wait_ge(s("lev_e"), i + 1)
                if i >= 1:
                    v.wait_ge(s("pt_done"), i + 1)
                e = halves((EB, EA)[i % 2], m)
                tt(halves(KH, m)[:, :, 0], halves(kO, m)[:, :, 0], e[:, :, 0], ALU.mult)
                tt(halves(QH, m)[:, :, 1], halves(qO, m)[:, :, 1], e[:, :, 1], ALU.mult).then_inc(s("qk_set"), 1)
                v.wait_ge(s("qk_set"), i + 1)
                pt_add(i)
            pt_add(6)
            v.memset(SG[0], 0.0).then_inc(s("sg_set"), 1)
            for c in range(NC - 1):
                v.wait_ge(s("sg_done"), c + 1)
                if c >= 1:
                    v.wait_ge(s("og_done"), c)
                v.wait_ge(s("sg_set"), 4 * c + 1)
                for h in range(4):
                    stt(out=SG[(c + 1) % 2][:, h], in0=SG[c % 2][:, h], scalar=elast[:, h, c:c + 1],
                        in1=ps[:, 2 + 2 * (c % 3) + h // 2, (h % 2) * 256:(h % 2) * 256 + 256], op0=ALU.mult, op1=ALU.add) \
                        .then_inc(s("sg_set"), 1)
            v.wait_ge(s("oproj_evac"), 29)
            for x in range(8):
                ins = v.tensor_scalar(rr[:, x], rr[:, x], col("gain", x), None, ALU.mult)
            link(ins)
            for h in range(4):
                v.wait_ge(s("og_rs"), h + 1)
                link(v.reciprocal(LA[:, h, 0:T], LA[:, h, 0:T]))
                for x in range(2):
                    link(tt(rr[:, 2 * h + x], rr[:, 2 * h + x], LA[:, h, 0:T], ALU.mult))
                    ins = tt(mixT[:, 2 * h + x], oG[:, 2 * h + x, PAD:TP], rr[:, 2 * h + x], ALU.mult)
            ins.then_inc(s("mix_ready"), 1)
            res_add(1)
            experts(1)
            v.wait_ge(s("ld_fn"), 16)
            v.wait_ge(s("y_sum"), 5)
            for n in range(2):
                v.wait_ge(s("hr_done"), n + 1)
                rows = yrow[:, n, 0].rearrange("p (d k) -> p k d", k=KD)
                for hf in range(2):
                    ins = tt(rows[:, 4 * hf:4 * hf + 4], rows[:, 4 * hf:4 * hf + 4],
                             ps[:, 2 * n + hf, :].rearrange("p (k d) -> p k d", k=4), ALU.add)
                ins.then_inc(s("fin_h"), 1)
            for n in range(2):
                v.wait_ge(s("fin_rs"), n + 1)
                link(v.reciprocal(fss[:, n:n + 1], fss[:, n:n + 1]))
                stt(out=yrow[:, n, 0], in0=yrow[:, n, 0], scalar=fss[:, n:n + 1], in1=fnb, op0=ALU.mult, op1=ALU.mult) \
                    .then_inc(s("out_set"), 1)


_INS = ['x', 'meta', 'e_norm', 'e_w_in', 'e_mu', 'e_decay0', 'e_decay_up', 'e_iclr0', 'e_iclr_up', 'e_gate_up', 'e_k_k',
        'e_k_a', 'e_r_k', 'e_ln_g', 'e_ln_b', 'e_conv_w', 'e_conv_b', 'e_lru_wa', 'e_lru_ba', 'e_lru_wx', 'e_lru_bx',
        'e_lru_lambda', 'e_w_out', 'o_norm', 'o_w_in', 'o_g_up', 'o_g_b', 'o_head_gain', 'o_w_out', 'm_norm',
        'm_w_group', 'm_b_group', 'm_w_router', 'm_b_router', 'm_w_gate', 'm_w_up', 'm_w_down', 'final_norm']


def kernel(**inputs):
    import numpy as _np
    import concourse.bacc as _bacc
    from concourse.bass_utils import run_bass_kernel_spmd as _run

    nc = _bacc.Bacc("TRN2", target_bir_lowering=False, num_devices=1)
    arrays, args = {}, {}
    for name in _INS:
        x = _np.ascontiguousarray(inputs[name])
        arrays[f"in_{name}_dram"] = x
        args[name] = nc.dram_tensor(f"in_{name}_dram", x.shape, mybir.dt.from_np(x.dtype), kind="ExternalInput").ap()
    out = nc.dram_tensor("out_0_dram", (1, SEQ, D), F32, kind="ExternalOutput").ap()
    y_rows = nc.dram_tensor("y_rows", (2 * T, D), F32).ap()
    program(nc, args, out, y_rows)
    r = _run(nc, [arrays], core_ids=[0])
    return r.results[0]["out_0_dram"]
```
